# Optimizing a Trainium2 kernel written in Bass

```python
import math
import jax
import jax.numpy as jnp
from jax import lax
import numpy as np

D_MODEL = 2048
BATCH = 1
SEQ = 256
DEPTH = 1

CTX_LEN = 256
GRID_W = 64
N_DELTA_HEADS = 8
HEAD_DIM = 128
D_DELTA = N_DELTA_HEADS * HEAD_DIM
D_CONV = D_MODEL - D_DELTA
SHORT_CONV_W = 5
CONFORMER_CONV_W = 31
CHUNK = 64
D_FF = -(-(8 * D_MODEL) // (3 * 256)) * 256
EPS = 1e-6
V_END = 3 * D_DELTA
STATE_END = V_END + 4 * N_DELTA_HEADS
Z_END = STATE_END + D_DELTA
D_IN = Z_END + 2 * D_CONV

kernel_name = "hybrid_deltanet_conformer_dit_layer"

def rms_norm(x, w):
    xf = x.astype(jnp.float32)
    y = xf * lax.rsqrt(jnp.mean(xf * xf, axis=-1, keepdims=True) + EPS)
    return (y * w.astype(jnp.float32)).astype(x.dtype)

def layer_norm(x, w, b):
    xf = x.astype(jnp.float32)
    mu = jnp.mean(xf, axis=-1, keepdims=True)
    var = jnp.mean(jnp.square(xf - mu), axis=-1, keepdims=True)
    y = (xf - mu) * lax.rsqrt(var + EPS) * w.astype(jnp.float32) + b.astype(jnp.float32)
    return y.astype(x.dtype)

def l2_normalize(x):
    xf = x.astype(jnp.float32)
    return xf * lax.rsqrt(jnp.sum(xf * xf, axis=-1, keepdims=True) + EPS)

def modulate(h, shift, scale):
    return h * (1 + scale) + shift

def depthwise_conv(u, w):
    pad = w.shape[0] // 2
    return lax.conv_general_dilated(
        u, w[:, None, :].astype(u.dtype), window_strides=(1,), padding=((pad, pad),),
        dimension_numbers=("NWC", "WIO", "NWC"), feature_group_count=u.shape[-1])

def split_heads(t):
    b, l, _ = t.shape
    return t.reshape(b, l, N_DELTA_HEADS, HEAD_DIM).transpose(0, 2, 1, 3)

def gated_delta_rule(q, k, v, beta, g, state0):
    b, h, l, dk = q.shape
    dv = v.shape[-1]
    n = l // CHUNK
    f32 = jnp.float32
    q = (q.astype(f32) * dk ** -0.5).reshape(b, h, n, CHUNK, dk)
    k = k.astype(f32).reshape(b, h, n, CHUNK, dk)
    v = v.astype(f32).reshape(b, h, n, CHUNK, dv)
    beta = beta.astype(f32).reshape(b, h, n, CHUNK)
    gcum = jnp.cumsum(g.astype(f32).reshape(b, h, n, CHUNK), axis=-1)
    pos = jnp.arange(CHUNK)
    incl = pos[:, None] >= pos[None, :]
    strict = pos[:, None] > pos[None, :]
    decay = jnp.exp(jnp.where(incl, gcum[..., :, None] - gcum[..., None, :], -jnp.inf))
    kb = k * beta[..., None]
    m = jnp.where(strict, jnp.einsum("bhncd,bhnsd->bhncs", kb, k) * decay, 0.0)
    eye = jnp.eye(CHUNK, dtype=f32)
    t_inv = lax.linalg.triangular_solve(eye + m, jnp.broadcast_to(eye, m.shape),
                                        left_side=True, lower=True, unit_diagonal=True)
    u = jnp.einsum("bhncs,bhnse->bhnce", t_inv, v * beta[..., None])
    w = jnp.einsum("bhncs,bhnsd->bhncd", t_inv, kb * jnp.exp(gcum)[..., None])
    attn = jnp.where(incl, jnp.einsum("bhncd,bhnsd->bhncs", q, k) * decay, 0.0)
    q_dec = q * jnp.exp(gcum)[..., None]
    k_dec = k * jnp.exp(gcum[..., -1:] - gcum)[..., None]
    chunk_decay = jnp.exp(gcum[..., -1])

    def step(state, inp):
        u_c, w_c, a_c, qd_c, kd_c, cd_c = inp
        v_new = u_c - jnp.einsum("bhcd,bhde->bhce", w_c, state)
        o_c = jnp.einsum("bhcd,bhde->bhce", qd_c, state) + jnp.einsum("bhcs,bhse->bhce", a_c, v_new)
        state = state * cd_c[..., None, None] + jnp.einsum("bhcd,bhce->bhde", kd_c, v_new)
        return state, o_c

    xs = tuple(jnp.moveaxis(t, 2, 0) for t in (u, w, attn, q_dec, k_dec, chunk_decay))
    state, o = lax.scan(step, state0.astype(f32), xs)
    return jnp.moveaxis(o, 0, 2).reshape(b, h, l, dv), state

def bidir_gated_delta(q, k, v, beta, g, state0):
    o_f, s_f = gated_delta_rule(q, k, v, beta[0], g[0], state0[0])
    rev = lambda t: jnp.flip(t, axis=2)
    o_b, s_b = gated_delta_rule(rev(q), rev(k), rev(v), rev(beta[1]), rev(g[1]), state0[1])
    return o_f + rev(o_b), jnp.stack([s_f, s_b])

def delta_inputs(p, conv_w, a_log, dt_bias):
    f32 = jnp.float32
    qkv = jax.nn.silu(depthwise_conv(p[..., :V_END], conv_w))
    q, k, v = jnp.split(qkv, 3, axis=-1)
    q, k, v = l2_normalize(split_heads(q)), l2_normalize(split_heads(k)), split_heads(v)
    b, l, _ = p.shape
    ba = p[..., V_END:STATE_END].astype(f32).reshape(b, l, 4, N_DELTA_HEADS)
    beta = jax.nn.sigmoid(ba[:, :, :2])
    g = -jnp.exp(a_log.astype(f32)) * jax.nn.softplus(ba[:, :, 2:] + dt_bias.astype(f32))
    return q, k, v, beta.transpose(2, 0, 3, 1), g.transpose(2, 0, 3, 1)

def delta_output(o, z, norm_w):
    y = rms_norm(o, norm_w) * jax.nn.silu(split_heads(z).astype(jnp.float32))
    b, h, l, d = y.shape
    return y.transpose(0, 2, 1, 3).reshape(b, l, h * d).astype(z.dtype)

def conformer_branch(p_glu, dw, ln_w, ln_b, n_rows):
    a, gate = jnp.split(p_glu, 2, axis=-1)
    u = a * jax.nn.sigmoid(gate)
    b, l, ch = u.shape
    u = depthwise_conv(u.reshape(b * n_rows, l // n_rows, ch), dw).reshape(b, l, ch)
    return jax.nn.silu(layer_norm(u, ln_w, ln_b))

def swiglu(h, w_gate, w_up, w_down):
    return (jax.nn.silu(h @ w_gate) * (h @ w_up)) @ w_down

def setup_inputs(seed: int = 0) -> dict:
    key = jax.random.key(seed)
    ks = jax.random.split(key, 24)
    f32 = jnp.float32
    nrm = lambda k, shape, s: jax.random.normal(k, shape, f32) * s
    gain = lambda k, shape: 1.0 + 0.02 * jax.random.normal(k, shape, f32)
    dt = jnp.exp(jax.random.uniform(ks[10], (DEPTH, 2, N_DELTA_HEADS), f32, math.log(1e-3), math.log(1e-1)))
    return {
        "x": nrm(ks[0], (BATCH, SEQ, D_MODEL), 1.0),
        "c": nrm(ks[1], (BATCH, D_MODEL), 1.0),
        "ctx": nrm(ks[2], (BATCH, CTX_LEN, D_MODEL), 1.0),
        "c_ctx": nrm(ks[3], (D_MODEL,), 1.0),
        "w_mod": nrm(ks[4], (DEPTH, D_MODEL, 6 * D_MODEL), 0.5 * D_MODEL ** -0.5),
        "b_mod": nrm(ks[5], (DEPTH, 6 * D_MODEL), 0.02),
        "mix_norm_pre": gain(ks[6], (DEPTH, D_MODEL)),
        "mix_norm_post": gain(ks[7], (DEPTH, D_MODEL)),
        "w_in": nrm(ks[8], (DEPTH, D_MODEL, D_IN), D_MODEL ** -0.5),
        "qkv_conv": nrm(ks[9], (DEPTH, SHORT_CONV_W, 3 * D_DELTA), SHORT_CONV_W ** -0.5),
        "a_log": jnp.log(jax.random.uniform(ks[11], (DEPTH, 2, N_DELTA_HEADS), f32, 1.0, 16.0)),
        "dt_bias": dt + jnp.log(-jnp.expm1(-dt)),
        "delta_out_norm": gain(ks[12], (DEPTH, HEAD_DIM)),
        "conf_dw": nrm(ks[13], (DEPTH, CONFORMER_CONV_W, D_CONV), CONFORMER_CONV_W ** -0.5),
        "conf_ln_w": gain(ks[14], (DEPTH, D_CONV)),
        "conf_ln_b": nrm(ks[15], (DEPTH, D_CONV), 0.02),
        "w_out": nrm(ks[16], (DEPTH, D_MODEL, D_MODEL), D_MODEL ** -0.5),
        "ffn_norm_pre": gain(ks[17], (DEPTH, D_MODEL)),
        "ffn_norm_post": gain(ks[18], (DEPTH, D_MODEL)),
        "w_gate": nrm(ks[19], (DEPTH, D_MODEL, D_FF), D_MODEL ** -0.5),
        "w_up": nrm(ks[20], (DEPTH, D_MODEL, D_FF), D_MODEL ** -0.5),
        "w_down": nrm(ks[21], (DEPTH, D_FF, D_MODEL), D_FF ** -0.5),
    }

def reference(x, c, ctx, c_ctx, w_mod, b_mod, mix_norm_pre, mix_norm_post, w_in, qkv_conv,
              a_log, dt_bias, delta_out_norm, conf_dw, conf_ln_w, conf_ln_b, w_out,
              ffn_norm_pre, ffn_norm_post, w_gate, w_up, w_down):
    n_lat = x.shape[1]
    rows = n_lat // GRID_W
    for i in range(DEPTH):
        last = i == DEPTH - 1
        mod = (jax.nn.silu(c) @ w_mod[i] + b_mod[i])[:, None, :]
        mod_c = jax.nn.silu(c_ctx) @ w_mod[i] + b_mod[i]
        sh1, sc1, g1, sh2, sc2, g2 = jnp.split(mod, 6, axis=-1)
        sh1c, sc1c, g1c, sh2c, sc2c, g2c = jnp.split(mod_c, 6, axis=-1)

        h = modulate(rms_norm(x, mix_norm_pre[i]), sh1, sc1)
        hc = modulate(rms_norm(ctx, mix_norm_pre[i]), sh1c, sc1c)
        p = h @ w_in[i]
        pc = hc @ (w_in[i][:, :STATE_END] if last else w_in[i])

        qc, kc, vc, bc, gc = delta_inputs(pc, qkv_conv[i], a_log[i], dt_bias[i])
        zero_state = jnp.zeros((2, ctx.shape[0], N_DELTA_HEADS, HEAD_DIM, HEAD_DIM), jnp.float32)
        o_c, s_ctx = bidir_gated_delta(qc, kc, vc, bc, gc, zero_state)
        q, k, v, bl, gl = delta_inputs(p, qkv_conv[i], a_log[i], dt_bias[i])
        o_lat, _ = bidir_gated_delta(q, k, v, bl, gl, s_ctx)

        mix = jnp.concatenate([
            delta_output(o_lat, p[..., STATE_END:Z_END], delta_out_norm[i]),
            conformer_branch(p[..., Z_END:], conf_dw[i], conf_ln_w[i], conf_ln_b[i], rows),
        ], axis=-1)
        x = x + g1 * rms_norm(mix @ w_out[i], mix_norm_post[i])
        if not last:
            mix_c = jnp.concatenate([
                delta_output(o_c, pc[..., STATE_END:Z_END], delta_out_norm[i]),
                conformer_branch(pc[..., Z_END:], conf_dw[i], conf_ln_w[i], conf_ln_b[i], 1),
            ], axis=-1)
            ctx = ctx + g1c * rms_norm(mix_c @ w_out[i], mix_norm_post[i])

        hf = modulate(rms_norm(x, ffn_norm_pre[i]), sh2, sc2)
        x = x + g2 * rms_norm(swiglu(hf, w_gate[i], w_up[i], w_down[i]), ffn_norm_post[i])
        if not last:
            hfc = modulate(rms_norm(ctx, ffn_norm_pre[i]), sh2c, sc2c)
            ctx = ctx + g2c * rms_norm(swiglu(hfc, w_gate[i], w_up[i], w_down[i]), ffn_norm_post[i])
    return x


_drawn_inputs = setup_inputs


def setup_inputs(seed=0):
    import zlib

    import numpy as np

    out = dict(_drawn_inputs(seed))
    spreads = {}
    factors = {'c_ctx': 3.967,
     'mix_norm_pre': 6.905,
     'mix_norm_post': 8.0,
     'delta_out_norm': 22.418,
     'conf_ln_w': 64.0,
     'conf_ln_b': 64.0,
     'ffn_norm_pre': 20.721,
     'ffn_norm_post': 33.372}
    for name, (base, spread) in spreads.items():
        noise = np.random.default_rng([zlib.crc32(name.encode()), seed]).standard_normal(out[name].shape)
        drawn = base * np.exp(spread * noise) if base else spread * noise
        out[name] = jnp.asarray(drawn.astype(out[name].dtype))
    for name, factor in factors.items():
        out[name] = (out[name] * factor).astype(out[name].dtype)
    return out
```

```python
from contextlib import ExitStack

import concourse.bass as bass
from concourse import mybir

F32 = mybir.dt.float32
F32R = mybir.dt.float32r
I32 = mybir.dt.int32
ALU = mybir.AluOpType
ACT = mybir.ActivationFunctionType
AX_X = mybir.AxisListType.X
ds = bass.ds

P = 128
D = 2048
KT = D // P
T = 256
NT = T // P
H = 8
NP = H // 2
ROW = 64
W5, W31 = 5, 31
DD = H * P
DC = D - DD
ST_END = 3 * DD + 4 * H
Z_END = ST_END + DD
DFF = 5632
FT = DFF // P
FC = DFF // 512
EPS = 1e-6
RING = 4
UN = 1024
LEVELS = 7
CTX, LAT, FFN = 0, 1, 2

VC_PRE1, VC_PRE2, VC_POST1, VC_POST2, VC_LNW, VC_LNB, VC_ON = 0, 16, 32, 48, 64, 72, 80
VC_MOD = 128
VC_C5 = 256
VC_C31 = 384

CU_COL = {"q": 0, "k": DD, "v": 2 * DD, "z": ST_END, "a": Z_END, "g": Z_END + DC}
CU_TILE = {"q": 0, "k": 8, "v": 16}
GATE_STEPS = ["bsig", "ny", "nex", "nln", "gg", "pref", "eall", "nbe"]

WINDOWS = [[("k", CTX, 0), ("v", CTX, 0)]] + [
    [("k", CTX, n), ("v", CTX, n), ("a", LAT, n - 1), ("g", LAT, n - 1)] for n in (1, 2, 3)] + [
    [("a", LAT, 3), ("g", LAT, 3), ("k", LAT, 0), ("v", LAT, 0), ("q", LAT, 0), ("z", LAT, 0)]] + [
    [("k", LAT, n), ("v", LAT, n), ("q", LAT, n), ("z", LAT, n)] for n in (1, 2, 3)]
CUS = [cu for w in WINDOWS for cu in w]
PAIRS = [(CTX, p) for p in range(NP)] + [(LAT, p) for p in range(NP)]
WO_FIRST = [(0, kg) for kg in range(4, 8)] + [(1, kg) for kg in range(4, 8)]
WO_REST = [(0, kg) for kg in range(4)] + [(1, kg) for kg in range(4)] + [
    (c, kg) for c in (2, 3) for kg in (4, 5, 6, 7, 0, 1, 2, 3)]


def delta_chunks(s, p):
    lat = s == LAT
    both = range(NT)
    ch = []
    for w in ("k", "q") if lat else ("k",):
        ch.append([("nsq", (s, w, p)), ("nrt", (s, w, p)), ("nrc", (s, w, p)), ("kn", (s, w, p))])
    ch.append([("kT", (s, p)), ("kTc", (s, p))])
    if lat:
        ch.append([("qT", (p, 0)), ("qTc", (p, 0)), ("qdec", (p, 1)), ("qT", (p, 1)), ("qTc", (p, 1)),
                   ("qdec", (p, 2)), ("qT", (p, 2)), ("qTc", (p, 2))])
    for t in both:
        ch.append([x for k in range(1 + lat) for x in (("gm", (s, p, t, k)), ("dec", (s, p, t, k)))]
                  + [("kk", (s, p, t)), ("edec", (s, p, t)), ("gk", (s, p, t)), ("mneg", (s, p, t)),
                     ("mhi", (s, p, t))] + ([("attn", (p, t))] if lat else []) + [("mk", (s, p, t, 0))])
    ch.append([("z", (s, p, t, 0)) for t in both])
    ch.append([x for t in both for x in (("xadd", (s, p, t, 0)), ("yadd", (s, p, t, 0)), ("mk", (s, p, t, 1)))])
    for l in range(1, LEVELS):
        ch.append([("z", (s, p, t, l)) for t in both])
        ch.append([(k, (s, p, t, l)) for k in ("zc", "xy") for t in both] + [x for t in both for x in (
            ("xadd", (s, p, t, l)), ("yadd", (s, p, t, l)),
            ("mk", (s, p, t, l + 1)) if l + 1 < LEVELS else ("mlo", (s, p, t)))])
    ch.append([("nr", (s, p, t)) for t in both])
    ch.append([x for t in both for x in (("nrr", (s, p, t)), ("nx", (s, p, t)))])
    ch.append([("xf", (s, p, t)) for t in both])
    for i in range(NT):
        first, last = (not lat and i == 0), (lat and i == 1)
        ch.append([("vb", (s, p, i))] + ([] if last else [("kd", (s, p, i))]) + ([] if first else [("ks", (s, p, i))]))
        ch.append(([] if first else [("r", (s, p, i))]) + [("vn", (s, p, i))])
        ch.append([("vnc", (s, p, i))] + ([] if last else [("st", (s, p, i)), ("stc", (s, p, i))]))
    if lat:
        ch.append([("o", (p,)), ("oc", (p,)), ("osq", (p,)), ("ort", (p,)), ("orc", (p,)), ("on", (p,))])
        ch.append([("oT", (p,)), ("ym", (p,)), ("mix_hi", (p,)), ("mix_lo", (p,))])
    return ch


def norm_chunks():
    ch = [[("lnm", ()), ("cen", ())]]
    ch += [[("csq", (i,)), ("lnv", (i,)), ("lva", (i,))] for i in range(4)]
    ch += [[("lsd", ()), ("lnr", ()), ("lnn", ())]]
    ch += [[("lny", (i,)), ("mix_hi", (NP + i,)), ("mix_lo", (NP + i,))] for i in range(4)]
    return ch


def evacuation(cu):
    what, s, p = cu
    if what in "kvq":
        return [("tap2", cu), ("taps", cu), ("csilu", cu), ("nat", cu), ("natc", cu)], []
    if what == "z":
        return [("zsilu", cu)], []
    if what == "a":
        return [], []
    return [("sg", (p,)), ("u", (p,))], [[("dw", (p, n))] for n in range(6)]


def turn_steps(s):
    return [(k, (s, kp)) for kp in range(8) for k in ("xT", "hf", "hhi", "hlo")]


def leaves_open(piece):
    for kind, key in piece:
        reads = [("xadd", key), ("yadd", key)] if kind == "xy" else [released_by(kind, key)]
        if any(r and r not in piece for r in reads):
            return True
    return False


def make_plan():
    plan = [("masks", ()), ("lvl", ()), ("cst", ()), ("vT", (0,)), ("vTc", (0,)), ("vT", (1,)), ("vTc", (1,)),
            ("csil", ()), ("c4h", ()), ("c4l", ()), ("nega", ())]
    ring = []
    mr = [("mr", m, j) for m in range(16) for j in range(8)]

    def unit(u, halves=1, beside=lambda: None):
        ring.append(u)
        plan.extend([("hi", (u,)), ("lo", (u,))])
        for half in range(halves):
            plan.append(("mm", (u, half)))
            beside()

    waiting = [[], 0]

    def place():
        plan.extend(waiting[0][waiting[1]])
        waiting[1] += 1

    def settle():
        while waiting[1] < len(waiting[0]) and waiting[1] and leaves_open(waiting[0][waiting[1] - 1]):
            place()

    def gates(n):
        for _ in range(n):
            if mr:
                x = mr.pop(0)
                ring.append(x)
                plan.append(("macc", x[1:]))
                if x[2] == 7:
                    settle()
                    plan.extend([("mcol", (x[1],)), ("mcc", (x[1],))])

    for half in range(2):
        for j in range(KT):
            for q in range(2):
                unit(("mod", half, j, q))
                if half == 0 and q == 1 and 2 <= j < 6:
                    s, t = divmod(j - 2, 2)
                    plan.append(("xsq", (s, t)))
                    if t == 1:
                        plan.extend([("xrt", (s,)), ("xrc", (s,)), ("xn", (s, 0)), ("xn", (s, 1))])
        plan.append(("mrow", (half,)))
    plan.extend([("modcol", ()), ("s1", ())])
    plan.extend(turn_steps(CTX))
    unit(("ba", CTX))
    plan.extend(turn_steps(LAT))
    plan.extend([(x, (CTX,)) for x in GATE_STEPS])
    for n, window in enumerate(WINDOWS):
        waiting[:] = [delta_chunks(*PAIRS[n - 1]) if n else [], 0]
        late = []
        slots = len(window) * 8
        done = [0]

        def beside():
            done[0] += 1
            while waiting[1] < len(waiting[0]) * done[0] // slots:
                place()
            if late:
                if any(released_by(*x) for x in late[0]):
                    settle()
                plan.extend(late.pop(0))

        for cu in window:
            for g in range(4):
                unit(("win", cu, g), 2, beside)
                if n:
                    gates(1 if g % 2 or len(mr) % 4 == 0 else 0)
            now, later = evacuation(cu)
            settle()
            plan.extend(now)
            late += later
            if cu == ("g", LAT, 3):
                late += norm_chunks()
            if cu == ("v", CTX, 0):
                unit(("ba", LAT))
                plan.extend([(x, (LAT,)) for x in GATE_STEPS])
        while waiting[1] < len(waiting[0]):
            place()
        for x in late:
            plan.extend(x)
    waiting[:] = [delta_chunks(LAT, 3), 0]
    done = [0]

    def beside():
        done[0] += 1
        while waiting[1] < len(waiting[0]) * done[0] // (2 * len(WO_FIRST)):
            place()

    for c, kg in WO_FIRST:
        unit(("wo", c, kg), 2, beside)
    gates(200)
    for q in range(4):
        plan.extend([("gdiag", (0, q)), ("gb", (0, q)), ("gbc", (0, q))])
    plan.append(("s2", ()))
    for c, kg in WO_REST:
        unit(("wo", c, kg), 2)
    for t in range(NT):
        plan.extend([("ysq", (t,)), ("yrt", (t,)), ("yrc", (t,))])
        plan.extend([(k, (t, c)) for c in range(4) for k in ("pn", "pa")])
        plan.extend([("xsq", (FFN, t))])
    plan.extend([("xrt", (FFN,)), ("xrc", (FFN,)), ("xnv", (0,)), ("xnv", (1,))])
    plan.extend(turn_steps(FFN))
    for q in range(4):
        plan.extend([("gdiag", (1, q)), ("gb", (1, q)), ("gbc", (1, q))])
    return plan, ring


def released_by(kind, key):
    if kind == "xy":
        return None
    return {
        "vT": ("vTc", key), "modcol": ("s1", ()), "xT": ("hf", key), "pref": ("eall", key), "nat": ("natc", key),
        "kT": ("kTc", key), "qT": ("qTc", key), "dec": ("edec", key[:3]), "kk": ("gk", key),
        "z": ("xadd" if key and key[-1] == 0 else "zc", key), "nr": ("nrr", key), "nx": ("xf", key),
        "ks": ("r", key), "vn": ("vnc", key), "st": ("stc", key), "o": ("oc", key), "oT": ("ym", key),
        "lnm": ("cen", ()), "lnv": ("lva", key), "mcol": ("mcc", key), "gb": ("gbc", key),
    }.get(kind)


def count_steps():
    plan, ring = make_plan()
    count, totals = {}, {}
    for kind, key in plan:
        assert (kind, key) not in count, (kind, key)
        totals[kind] = totals.get(kind, 0) + 1
        count[kind, key] = totals[kind]
    aux, bank, before = [], {}, {}
    place = {step: n for n, step in enumerate(plan)}
    for kind, key in plan:
        if kind == "dec" and key[3] == 1:
            continue
        if kind == "xy":
            uses = [((kind, key, "x"), ("xadd", key)), ((kind, key, "y"), ("yadd", key))]
        else:
            r = released_by(kind, key)
            uses = [((kind, key), r)] if r else []
        for use, release in uses:
            n = len(aux)
            bank[use] = 4 + n % 4
            before[use] = aux[n - 4] if n >= 4 else None
            assert n < 4 or place[aux[n - 4]] < place[kind, key], (kind, key, aux[n - 4])
            aux.append(release)
    return plan, ring, count, totals, bank, before


def layer(nc, x, cond, ctx, c_ctx, w_mod, b_mod, mix_norm_pre, mix_norm_post, w_in, qkv_conv, a_log, dt_bias,
          delta_out_norm, conf_dw, conf_ln_w, conf_ln_b, w_out, ffn_norm_pre, ffn_norm_post, w_gate, w_up,
          w_down, out):
    PLAN, RINGED, COUNT, TOTALS, BANK, BEFORE = count_steps()
    at_ring = {u: n for n, u in enumerate(RINGED)}

    es = ExitStack()
    with es:
        def alloc(stack):
            return lambda name, shape, dt=F32: stack.enter_context(nc.sbuf_tensor(name, [P, *shape], dt))

        sb = alloc(es)
        h_hi = sb("h_hi", [KT, T], F32R)
        h_lo = sb("h_lo", [KT, T], F32R)
        raw = sb("raw", [RING, UN])
        w_hi = sb("w_hi", [RING, UN], F32R)
        w_lo = sb("w_lo", [RING, UN], F32R)
        ident = sb("ident", [P])
        ones = sb("ones", [P])
        vcol = sb("vcol", [632])
        sh1 = sb("sh1", [KT, 2])
        sc1 = sb("sc1", [KT, 2])
        sc2 = sb("sc2", [KT])
        modc = sb("modc", [64])
        gw = sb("gw", [2, KT])
        csil = sb("csil", [2, KT])
        cst = sb("cst", [4])
        sums = sb("sums", [16])
        rstd = sb("rstd", [16])
        rtmp = sb("rtmp", [16])

        with ExitStack() as mixer:
            mb = alloc(mixer)
            hc_hi = mb("hc_hi", [KT, T], F32R)
            hc_lo = mb("hc_lo", [KT, T], F32R)
            mhi = mb("mhi", [NT, 4, P], F32R)
            mkl = mb("mkl", [NT, 4, P], F32R)
            xi = mb("xi", [NT, 4, P], F32R)
            yi = mb("yi", [NT, 4, P], F32R)
            zi = mb("zi", [NT, 4, P], F32R)
            id_r = mb("id_r", [P], F32R)
            nid_r = mb("nid_r", [P], F32R)
            c4 = mb("c4", [KT, 4], F32R)
            m_le, m_ge, m_lt, m_gt = (mb(f"m_{n}", [P]) for n in ("le", "ge", "lt", "gt"))
            lvl = mb("lvl", [LEVELS, P])
            gates_ = {s: {n: mb(f"{n}{s}", [2, NT, H]) for n in ("beta", "g", "nbeta", "y0", "y1", "y2")}
                      for s in (CTX, LAT)}
            ex = [mb(f"ex{s}", [3, 2, NT, H]) for s in (CTX, LAT)]
            nega = mb("nega", [16])
            dtb = mb("dtb", [16])
            macc = mb("macc", [512])
            cx = mb("cx", [2, T])
            with ExitStack() as start:
                st = alloc(start)
                xs = [st("xs_ctx", [NT, D]), st("xs_lat", [NT, D])]
                modrow = st("modrow", [2 * D])
                hfs = st("hfs", [2, 2, T])
                vnat = st("vnat", [5, P])
                sel = st("sel", [2])
                ix = st("ix", [2, P], I32)
                lt = st("lt", [P])
            kvq = {w: mb(f"{w}n", [2, NT, 2, P]) for w in "kvq"}
            kTs = mb("kTs", [NT, 2, P])
            sil = mb("sil", [2, 2, T])
            zs = mb("zs", [2, 2, T])
            e_ = mb("e_", [4, P])
            mn = mb("mn", [NT, 4, P])
            sctx = mb("sctx", [NP, 4, P])
            vnew = mb("vnew", [NT, 4, P])
            rb = mb("rb", [4, P])
            kd = mb("kd", [4, P])
            gmv, tmp = kd[:, :, :].rearrange("p (d h) c -> p d h c", d=2), kd[:, :, :].rearrange("p a b -> p (a b)")
            with ExitStack() as conf:
                cf = alloc(conf)
                cacc = cf("cacc", [8, T])
                sgb = cf("sgb", [512])
                ub = cf("ub", [512])
            qx = mb("qx", [NT, 2, P])
            qTs = mb("qTs", [3, NT, 2, P])
            at = mb("at", [NT, 2, 2, P])
            slat = mb("slat", [4, P])
        act_hi = sb("act_hi", [FT, T], F32R)
        with ExitStack() as pre:
            xn2 = alloc(pre)("xn2", [NT, D])
            hf2 = alloc(pre)("hf2", [2, 2, T])
            junk2 = alloc(pre)("junk2", [D])
        act_lo = sb("act_lo", [FT, T], F32R)
        x1 = sb("x1", [NT, D])
        g1w = sb("g1w", [D])
        sgf = sb("sgf", [NT, 512])
        anf = sb("anf", [NT, 512])
        g2w = g1w

        PS = es.enter_context(nc.psum_tensor("PS", [P, 8, 512], F32))

        def sem(name):
            return es.enter_context(nc.semaphore(name))

        S = {kind: sem(f"s_{kind}") for kind in TOTALS}
        landed = [sem(f"landed{i}") for i in range(RING)]
        small_in = {n: sem(f"in_{n}") for n in ("vec", "c", "dt", "bmod", "x0", "x1")}
        x_again, out_done = sem("x_again"), sem("out_done")
        ch_pool, ch_dve = sem("ch_pool"), sem("ch_dve")
        f_mm, f_sg, f_an, f_tr, f_ah, f_al, f_sq, f_yg, f_rt, f_rc, f_out = (
            sem(f"f_{n}") for n in ("mm", "sg", "an", "tr", "ah", "al", "sq", "yg", "rt", "rc", "out"))

        def need(eng, kind, *key):
            eng.wait_ge(S[kind], COUNT[kind, key])

        def bc(ap, axis, n):
            ap = ap.unsqueeze(axis)
            shape = list(ap.shape)
            shape[axis] = n
            return ap.to_broadcast(shape)

        def aux(eng, kind, key, part=None):
            use = (kind, key) if part is None else (kind, key, part)
            if BEFORE[use]:
                need(eng, BEFORE[use][0], *BEFORE[use][1])
            return BANK[use]

        def first_read(what):
            if what[0] == "ba":
                return [("bsig", what[1:]), ("ny", what[1:])]
            return {"a": [("u", what[2:])], "g": [("sg", what[2:])], "z": [("zsilu", what)]}.get(
                what[0], [("taps", what)])

        projected = []
        for u in RINGED:
            if u[0] == "ba" or (u[0] == "win" and u[2] == 0):
                projected.append(u if u[0] == "ba" else u[1])
        proj_bank = {w: n % 4 for n, w in enumerate(projected)}
        last_unit = {w: (w, 0) if w[0] == "ba" else (("win", w, 3), 1) for w in projected}
        conv_cus = [cu for cu in CUS if cu[0] in "kvq"]
        split_before = {}
        for n, u in enumerate(RINGED):
            k = n - RING
            while k >= 0 and RINGED[k][0] == "mr":
                k -= RING
            split_before[u] = RINGED[k] if k >= 0 else None

        def last_mm(u):
            return (u, 1) if u[0] in ("win", "wo") else (u, 0)

        def projection(eng, what):
            need(eng, "mm", *last_unit[what])
            return PS[:, proj_bank[what], :]

        def unit_size(u):
            return KT * 4 * H if u[0] == "ba" else UN

        def wide(u, n):
            return w_hi[:, at_ring[u] % RING, 0:n], w_lo[:, at_ring[u] % RING, 0:n]

        w_mod_v = w_mod[0].rearrange("(p j) n -> p j n", j=KT)
        w_in_v = w_in[0].rearrange("(k p) n -> p k n", p=P)
        w_out_v = w_out[0].rearrange("(k p) n -> p k n", p=P)
        w_gate_v = w_gate[0].rearrange("(k p) n -> p k n", p=P)
        w_up_v = w_up[0].rearrange("(k p) n -> p k n", p=P)
        w_down_v = w_down[0].rearrange("(k p) n -> p k n", p=P)
        x_v = x[0].rearrange("(t p) n -> p t n", p=P)
        out_v = out[0].rearrange("(t p) n -> p t n", p=P)

        def unit_source(u):
            if u[0] == "mod":
                _, half, j, q = u
                return w_mod_v[:, j, half * D + q * UN:half * D + (q + 1) * UN]
            if u[0] == "ba":
                return w_in_v[:, :, 3 * DD:ST_END]
            if u[0] == "win":
                (what, _, p), g = u[1:]
                col = CU_COL[what] + 256 * p
                return w_in_v[:, 4 * g:4 * g + 4, col:col + 256]
            if u[0] == "wo":
                return w_out_v[:, 2 * u[2]:2 * u[2] + 2, 512 * u[1]:512 * (u[1] + 1)]
            return w_mod_v[:, 2 * u[2]:2 * u[2] + 2, 2 * D + 512 * u[1]:2 * D + 512 * (u[1] + 1)]

        def tile_of(d, i):
            return i if d == 0 else 1 - i

        R0, B0 = len(RINGED), TOTALS["hi"]
        NG = FC * 16
        ND = 4 * (FT // 2)

        seq_h = {CTX: (hc_hi, hc_lo), LAT: (h_hi, h_lo), FFN: (h_hi, h_lo)}

        block = es.enter_context(nc.Block())

        @block.sync
        def _(sp):
            sp.dma_start(csil[:, CTX, :], c_ctx.rearrange("(p j) -> p j", j=KT)).then_inc(small_in["c"], 16)
            sp.dma_start(csil[:, LAT, :], cond[0].rearrange("(p j) -> p j", j=KT)).then_inc(small_in["c"], 16)
            for n, u in enumerate(RINGED):
                if n >= RING:
                    old = RINGED[n - RING]
                    if old[0] == "mr":
                        need(sp, "macc", *old[1:])
                    else:
                        need(sp, "hi", old)
                        need(sp, "lo", old)
                src = unit_source(u)
                dst = raw[:, n % RING, 0:unit_size(u)]
                if len(src.shape) == 3:
                    dst = dst.rearrange("p (a b) -> p a b", a=src.shape[1])
                sp.dma_start(dst, src).then_inc(landed[n % RING], 16)
                if n == 8:
                    for s, a in ((0, ctx), (1, x)):
                        sp.dma_start(xs[s][:, :, :], a[0].rearrange("(t p) n -> p t n", p=P)).then_inc(
                            small_in[f"x{s}"], 16)
                if u == ("wo",) + WO_REST[0]:
                    need(sp, "mix_lo", NP - 1)
                    sp.dma_start(x1[:, :, :], x_v).then_inc(x_again, 16)

            def load(U, src):
                sp.wait_ge(S["hi"], B0 + U - RING + 1)
                sp.wait_ge(S["lo"], B0 + U - RING + 1)

            def gate_up(c, c16):
                for i in range(16):
                    sp.wait_ge(S["hi"], B0 - RING + 1 + i + c16)
                    sp.wait_ge(S["lo"], B0 - RING + 1 + i + c16)
                    src = w_gate_v if i < 8 else w_up_v
                    k = 2 * (i % 8)
                    cols = slice(c * 512, (c + 1) * 512) if isinstance(c, int) else ds(c * 512, 512)
                    sp.dma_start(raw[:, (R0 + i) % RING, :].rearrange("p (a b) -> p a b", a=2),
                                 src[:, k:k + 2, cols]).then_inc(landed[(R0 + i) % RING], 16)

            gate_up(0, 0)
            with sp.Fori(1, FC) as c:
                gate_up(c, c * 16)
            for v in range(ND):
                U = NG + v
                sp.wait_ge(S["hi"], B0 + U - RING + 1)
                sp.wait_ge(S["lo"], B0 + U - RING + 1)
                cc, g = divmod(v, FT // 2)
                sp.dma_start(raw[:, (R0 + U) % RING, :].rearrange("p (a b) -> p a b", a=2),
                             w_down_v[:, 2 * g:2 * g + 2, 512 * cc:512 * (cc + 1)]).then_inc(
                    landed[(R0 + U) % RING], 16)
            for n in range(8):
                t, cc = divmod(n, 4)
                sp.wait_ge(f_out, n + 1)
                sp.dma_start(out_v[:, t, 512 * cc:512 * (cc + 1)], x1[:, t, 512 * cc:512 * (cc + 1)]).then_inc(
                    out_done, 16)
            sp.wait_ge(out_done, 16 * 8)

        @block.gpsimd
        def _(pool):
            n_chain = [0]

            def link(ins):
                n_chain[0] += 1
                ins.then_inc(ch_pool, 1)
                pool.wait_ge(ch_pool, n_chain[0])

            def masks():
                pool.memset(sel[:, :], 0.0)
                pool.memset(ident[:, :], 0.0)
                link(pool.memset(ones[:, :], 1.0))
                pool.iota(ix[:, 0, :], [[0, P]], base=0, channel_multiplier=1)
                pool.iota(ix[:, 1, :], [[1, P]], base=0, channel_multiplier=0)
                for m, sign, op in ((m_le, 1, ALU.is_ge), (m_lt, 1, ALU.is_gt), (m_ge, -1, ALU.is_ge),
                                    (m_gt, -1, ALU.is_gt)):
                    pool.affine_select(out=m[:, :], in_=ones[:, :], compare_op=op, fill=0.0, base=0,
                                       pattern=[[sign, P]], channel_multiplier=-sign)
                pool.affine_select(out=ident[:, :], in_=ident[:, :], compare_op=ALU.not_equal, fill=1.0, base=0,
                                   pattern=[[-1, P]], channel_multiplier=1)
                for base, step in ((0, -1), (-2, -1)):
                    link(pool.affine_select(out=sel[:, :], in_=sel[:, :], compare_op=ALU.not_equal, fill=1.0,
                                            base=base, pattern=[[step, 2]], channel_multiplier=1))
                pool.affine_select(out=sel[:, :], in_=sel[:, :], compare_op=ALU.not_equal, fill=1.0, base=-4,
                                   pattern=[[0, 2]], channel_multiplier=1).then_inc(S["masks"], 1)

            def small_loads():
                for r, (v, n) in enumerate(((mix_norm_pre, 16), (ffn_norm_pre, 16), (mix_norm_post, 16),
                                            (ffn_norm_post, 16), (conf_ln_w, 8), (conf_ln_b, 8),
                                            (delta_out_norm, 1))):
                    row = (0, 16, 32, 48, 64, 72, 80)[r]
                    pool.dma_start(vnat[row:row + n, 0, :], v[0].rearrange("(a b) -> a b", b=P)).then_inc(
                        small_in["vec"], 16)
                pool.dma_start(vnat[0:64, 1, :], b_mod[0, 2 * D:6 * D].rearrange("(a b) -> a b", b=P)).then_inc(
                    small_in["vec"], 16)
                pool.dma_start(vnat[0:120, 2, :], qkv_conv[0].rearrange("w (a b) -> (w a) b", b=P)).then_inc(
                    small_in["vec"], 16)
                dw = conf_dw[0].rearrange("w (a b) -> (w a) b", b=P)
                pool.dma_start(vnat[0:124, 3, :], dw[0:124, :]).then_inc(small_in["vec"], 16)
                pool.dma_start(vnat[0:124, 4, :], dw[124:248, :]).then_inc(small_in["vec"], 16)
                pool.dma_start(nega[:, :], a_log[0].rearrange("a b -> (a b)").partition_broadcast(P)).then_inc(
                    small_in["dt"], 16)
                pool.dma_start(dtb[:, :], dt_bias[0].rearrange("a b -> (a b)").partition_broadcast(P)).then_inc(
                    small_in["dt"], 16)
                pool.dma_start(modrow[4:5, :], b_mod[0:1, 0:2 * D]).then_inc(small_in["bmod"], 16)

            small_loads()
            for kind, key in PLAN:
                if kind == "masks":
                    masks()
                elif kind == "xn":
                    s, t = key
                    need(pool, "xrc", s)
                    pool.tensor_scalar(xs[s][:, t, :], xs[s][:, t, :], rstd[:, 2 * s + t:2 * s + t + 1], None,
                                       ALU.mult).then_inc(S[kind], 1)
                elif kind == "gm":
                    s, p, t, k = key
                    need(pool, "gg", s)
                    if (t, k) != (0, 0):
                        pool.wait_ge(S["dec"], COUNT["gm", key] - 1)
                    else:
                        need(pool, "nsq", s, "q" if s == LAT else "k", p)
                    for d, m in enumerate(((m_gt, m_lt), (m_le, m_ge))[k]):
                        ins = pool.tensor_tensor(gmv[:, d, :, :], bc(m[:, :], 1, 2),
                                                 bc(gates_[s]["g"][:, d, t, 2 * p:2 * p + 2], 2, P), ALU.mult)
                    ins.then_inc(S[kind], 1)
                elif kind == "qdec":
                    p, k = key
                    need(pool, "kn", LAT, "q", p)
                    need(pool, "eall", LAT)
                    if k == 2:
                        need(pool, "qT", p, 1)
                    elif p:
                        need(pool, "qT", p - 1, 2)
                    else:
                        need(pool, "mix_lo", NP + 3)
                    par = PAIRS.index((LAT, p)) % 2
                    pool.tensor_tensor(qx[:, :, :, :], kvq["q"][:, par, :, :, :],
                                       bc(ex[LAT][:, 0, k - 1, :, 2 * p:2 * p + 2], 3, P), ALU.mult).then_inc(S[kind], 1)
                elif kind == "attn":
                    p, t = key
                    need(pool, "gk", LAT, p, t)
                    if p:
                        need(pool, "o", p - 1)
                    else:
                        need(pool, "mix_lo", NP + 3)
                    for d, m in enumerate((m_le, m_ge)):
                        ins = pool.tensor_tensor(at[:, t, d, :, :], e_[:, 2:4, :], bc(m[:, :], 1, 2), ALU.mult)
                    ins.then_inc(S[kind], 1)
                elif kind == "mk":
                    s, p, t, l = key
                    need(pool, "mhi", s, p, t)
                    need(pool, "lvl")
                    if l:
                        need(pool, "z", s, p, t, l - 1)
                        if l == 1:
                            need(pool, "yadd", s, p, t, 0)
                    elif (s, p) != PAIRS[0]:
                        need(pool, "nr", *PAIRS[PAIRS.index((s, p)) - 1], t)
                    pool.tensor_tensor(mkl[:, t, :, :], mhi[:, t, :, :].bitcast(F32), bc(lvl[:, l, :], 1, 4),
                                       ALU.mult).then_inc(S[kind], 1)
                elif kind == "mlo":
                    s, p, t = key
                    need(pool, "z", s, p, t, LEVELS - 1)
                    need(pool, "mneg", s, p, t)
                    pool.tensor_tensor(mkl[:, t, :, :], mn[:, t, :, :], mhi[:, t, :, :].bitcast(F32),
                                       ALU.subtract).then_inc(S[kind], 1)
                elif kind == "vb":
                    s, p, i = key
                    par = PAIRS.index((s, p)) % 2
                    need(pool, "natc", "v", s, p)
                    need(pool, "bsig", s)
                    if (s, p, i) != (CTX, 0, 0):
                        prev = (s, p, i - 1) if i else (*PAIRS[PAIRS.index((s, p)) - 1], 1)
                        need(pool, "vn", *prev)
                        if i == 0 and prev[0] == LAT:
                            need(pool, "oT", prev[1])
                    for d in range(2):
                        ins = pool.tensor_tensor(rb[:, 2 * d:2 * d + 2, :], kvq["v"][:, par, tile_of(d, i), :, :],
                                                 bc(gates_[s]["beta"][:, d, tile_of(d, i), 2 * p:2 * p + 2], 2, P),
                                                 ALU.mult)
                    ins.then_inc(S[kind], 1)
                elif kind == "kd":
                    s, p, i = key
                    par = PAIRS.index((s, p)) % 2
                    need(pool, "kn", s, "k", p)
                    need(pool, "eall", s)
                    if i:
                        need(pool, "st", s, p, 0)
                    else:
                        need(pool, "dec", s, p, 1, 1 if s == LAT else 0)
                    for d in range(2):
                        ins = pool.tensor_tensor(kd[:, 2 * d:2 * d + 2, :], kvq["k"][:, par, tile_of(d, i), :, :],
                                                 bc(ex[s][:, 1, d, tile_of(d, i), 2 * p:2 * p + 2], 2, P), ALU.mult)
                    ins.then_inc(S[kind], 1)
                elif kind == "pa":
                    t, cc = key
                    need(pool, "pn", t, cc)
                    pool.wait_ge(x_again, 16)
                    xc = x1[:, t, 512 * cc:512 * (cc + 1)]
                    pool.tensor_tensor(xc, xc, anf[:, cc % 2, :], ALU.add).then_inc(S[kind], 1)

        @block.scalar
        def _(act):
            def copy(out_ap, in_ap, kind):
                act.activation(out_ap, in_ap, ACT.Copy).then_inc(S[kind], 1)

            for kind, key in PLAN:
                if kind == "vTc":
                    n, = key
                    need(act, "vT", n)
                    b = BANK["vT", key]
                    if n == 0:
                        act.activation(vcol[:, 0:81], PS[:, b, 0:81], ACT.Copy)
                        act.activation(vcol[:, VC_MOD:VC_MOD + 64], PS[:, b, 128:192], ACT.Copy)
                        copy(vcol[:, VC_C5:VC_C5 + 120], PS[:, b, 256:376], kind)
                    else:
                        copy(vcol[:, VC_C31:VC_C31 + 248], PS[:, b, 0:248], kind)
                elif kind == "csil":
                    act.wait_ge(small_in["c"], 32)
                    act.activation(csil[:, :, :], csil[:, :, :], ACT.Silu).then_inc(S[kind], 1)
                elif kind == "c4h":
                    need(act, "csil")
                    copy(c4[:, :, 0:2].rearrange("p j w -> p w j"), csil[:, :, :], kind)
                elif kind == "nega":
                    act.wait_ge(small_in["dt"], 32)
                    act.activation(nega[:, :], nega[:, :], ACT.Exp).then_inc(S[kind], 1)
                elif kind == "hi":
                    u, = key
                    n = at_ring[u]
                    act.wait_ge(landed[n % RING], 16 * (n // RING + 1))
                    if split_before[u]:
                        need(act, "mm", *last_mm(split_before[u]))
                    sz = unit_size(u)
                    copy(wide(u, sz)[0], raw[:, n % RING, 0:sz], kind)
                elif kind == "xsq":
                    s, t = key
                    if s == FFN:
                        need(act, "pa", t, 3)
                        if t:
                            need(act, "xsq", FFN, 0)
                        act.activation(junk2[:, :], x1[:, t, :], ACT.Square,
                                       accum_out=sums[:, 4 + t:5 + t]).then_inc(S[kind], 1)
                    else:
                        act.wait_ge(small_in[f"x{s}"], 16)
                        if (s, t) == (0, 0):
                            need(act, "vTc", 1)
                        else:
                            act.wait_ge(S[kind], 2 * s + t)
                        act.activation(PS[:, 4:8, :].rearrange("p a b -> p (a b)"), xs[s][:, t, :], ACT.Square,
                                       accum_out=sums[:, 2 * s + t:2 * s + t + 1]).then_inc(S[kind], 1)
                elif kind == "xrt":
                    s, = key
                    need(act, "xsq", s, 1)
                    need(act, "cst")
                    act.activation(rtmp[:, 2 * s:2 * s + 2], sums[:, 2 * s:2 * s + 2], ACT.Sqrt, bias=cst[:, 0:1],
                                   scale=1.0 / D).then_inc(S[kind], 1)
                elif kind == "mrow":
                    half, = key
                    need(act, "mm", ("mod", half, KT - 1, 1), 0)
                    copy(modrow[0:4, half * D:(half + 1) * D], PS[0:4, 0:4, :].rearrange("p a b -> p (a b)"), kind)
                elif kind == "hhi":
                    s, kp = key
                    need(act, "hf", s, kp)
                    buf = hf2 if s == FFN else hfs
                    copy(seq_h[s][0][:, 2 * kp:2 * kp + 2, :], buf[:, kp % 2, :, :], kind)
                elif kind == "bsig":
                    s, = key
                    pr = projection(act, ("ba", s))[:, 0:64].rearrange("p (t n) -> p t n", t=NT)
                    for d in range(2):
                        ins = act.activation(gates_[s]["beta"][:, d, :, :], pr[:, :, 8 * d:8 * d + 8], ACT.Sigmoid)
                    ins.then_inc(S[kind], 1)
                elif kind == "nex":
                    s, = key
                    need(act, "ny", s)
                    y2 = gates_[s]["y2"][:, :, :, :]
                    act.activation(y2, y2, ACT.Exp).then_inc(S[kind], 1)
                elif kind == "nln":
                    s, = key
                    need(act, "nex", s)
                    y2 = gates_[s]["y2"][:, :, :, :]
                    act.activation(y2, y2, ACT.Ln, bias=cst[:, 2:3]).then_inc(S[kind], 1)
                elif kind == "eall":
                    s, = key
                    need(act, "pref", s)
                    act.activation(ex[s][:, :, :, :, :].rearrange("p a b c d -> p (a b c d)"),
                                   PS[:, BANK["pref", key], 0:96], ACT.Exp).then_inc(S[kind], 1)
                elif kind == "tap2":
                    n = conv_cus.index(key)
                    what, s, p = key
                    pr = projection(act, key)
                    if n >= 2:
                        need(act, "nat", *conv_cus[n - 2])
                    else:
                        need(act, "hlo", LAT, 7)
                    for h in range(2):
                        col = VC_C5 + 2 * 24 + CU_TILE[what] + 2 * p + h
                        ins = act.activation(sil[:, n % 2, h, :], pr[:, T * h:T * (h + 1)], ACT.Copy,
                                             scale=vcol[:, col:col + 1])
                    ins.then_inc(S[kind], 1)
                elif kind == "csilu":
                    n = conv_cus.index(key)
                    need(act, "taps", *key)
                    act.activation(sil[:, n % 2, :, :], sil[:, n % 2, :, :], ACT.Silu).then_inc(S[kind], 1)
                elif kind == "natc":
                    what, s, p = key
                    need(act, "nat", *key)
                    k = PAIRS.index((s, p))
                    if k >= 2:
                        need(act, "vb", *PAIRS[k - 2], 1)
                    copy(kvq[what][:, k % 2, :, :, :].rearrange("p t h d -> p (t h d)"),
                         PS[:, BANK["nat", key], :], kind)
                elif kind == "zsilu":
                    p = key[2]
                    pr = projection(act, key)
                    if p >= 2:
                        need(act, "ym", p - 2)
                    act.activation(zs[:, p % 2, :, :].rearrange("p h t -> p (h t)"), pr, ACT.Silu).then_inc(S[kind], 1)
                elif kind == "nrt":
                    s, what, p = key
                    need(act, "nsq", *key)
                    a = 8 if what == "k" else 12
                    act.activation(rtmp[:, a:a + 4], sums[:, a:a + 4], ACT.Sqrt,
                                   bias=cst[:, 0:1] if what == "k" else cst[:, 1:2],
                                   scale=1.0 if what == "k" else float(P)).then_inc(S[kind], 1)
                elif kind == "kTc":
                    need(act, "kT", *key)
                    k = PAIRS.index(key)
                    if k:
                        need(act, "ks", *PAIRS[k - 1], 1)
                    copy(kTs[:, :, :, :].rearrange("p t h d -> p (t h d)"), PS[:, BANK["kT", key], :], kind)
                elif kind == "qTc":
                    p, k = key
                    need(act, "qT", p, k)
                    if p:
                        need(act, "o", p - 1)
                    copy(qTs[:, k, :, :, :].rearrange("p t h d -> p (t h d)"), PS[:, BANK["qT", key], :], kind)
                elif kind == "edec":
                    s, p, t = key
                    n = 4 if s == LAT else 2
                    need(act, "dec", s, p, t, n // 2 - 1)
                    if COUNT[kind, key] > 1:
                        act.wait_ge(S["mneg"], COUNT[kind, key] - 1)
                        if s == LAT and (p, t) != (0, 0):
                            need(act, "attn", *((p, 0) if t else (p - 1, 1)))
                    act.activation(e_[:, 0:n, :].rearrange("p a b -> p (a b)"),
                                   PS[:, BANK["dec", (s, p, t, 0)], 0:n * P], ACT.Exp).then_inc(S[kind], 1)
                elif kind == "mhi":
                    s, p, t = key
                    need(act, "mneg", s, p, t)
                    if (s, p) != PAIRS[0]:
                        need(act, "nr", *PAIRS[PAIRS.index((s, p)) - 1], t)
                    copy(mhi[:, t, :, :], mn[:, t, :, :], kind)
                elif kind == "zc":
                    t = key[2]
                    need(act, "z", *key)
                    k = PAIRS.index(key[:2])
                    if key[3] == 1 and k:
                        need(act, "nx", *PAIRS[k - 1], t)
                    copy(zi[:, t, :, :].rearrange("p a b -> p (a b)"), PS[:, BANK["z", key], :], kind)
                elif kind == "vnc":
                    s, p, i = key
                    need(act, "vn", *key)
                    if s == LAT and p:
                        need(act, "o", p - 1)
                    copy(vnew[:, i, :, :].rearrange("p a b -> p (a b)"), PS[:, BANK["vn", key], :], kind)
                elif kind == "oc":
                    need(act, "o", *key)
                    copy(rb[:, :, :].rearrange("p a b -> p (a b)"), PS[:, BANK["o", key], :], kind)
                elif kind == "ort":
                    need(act, "osq", *key)
                    act.activation(rtmp[:, 8:12], sums[:, 8:12], ACT.Sqrt, bias=cst[:, 0:1],
                                   scale=1.0 / P).then_inc(S[kind], 1)
                elif kind == "mix_hi":
                    n, = key
                    if n < NP:
                        need(act, "ym", n)
                        src = kd[:, :, :].rearrange("p a b -> p (a b)")
                    else:
                        need(act, "lny", n - NP)
                        src = ub[:, :]
                    if n == NP:
                        need(act, "mm", ("win", ("v", CTX, 3), 3), 1)
                    copy(hc_hi[:, 2 * n:2 * n + 2, :].rearrange("p a b -> p (a b)"), src, kind)
                elif kind == "sg":
                    i, = key
                    pr = projection(act, ("g", LAT, i))
                    if i:
                        need(act, "u", i - 1)
                    act.activation(sgb[:, :], pr, ACT.Sigmoid).then_inc(S[kind], 1)
                elif kind == "csq":
                    i, = key
                    if i:
                        need(act, "lnv", i - 1)
                    need(act, "cen")
                    act.activation(ub[:, :], cacc[:, 2 * i:2 * i + 2, :].rearrange("p a b -> p (a b)"),
                                   ACT.Square).then_inc(S[kind], 1)
                elif kind == "lsd":
                    need(act, "lva", 3)
                    act.activation(cx[:, 1, :], cx[:, 0, :], ACT.Sqrt, bias=cst[:, 0:1],
                                   scale=1.0 / DC).then_inc(S[kind], 1)
                elif kind == "lny":
                    i, = key
                    need(act, "lnn")
                    if i:
                        need(act, "mix_hi", NP + i - 1)
                        need(act, "mix_lo", NP + i - 1)
                    for h in range(2):
                        n = 2 * i + h
                        ins = act.activation(ub[:, T * h:T * (h + 1)], cacc[:, n, :], ACT.Silu,
                                             scale=vcol[:, VC_LNW + n:VC_LNW + n + 1],
                                             bias=vcol[:, VC_LNB + n:VC_LNB + n + 1])
                    ins.then_inc(S[kind], 1)
                elif kind == "gbc":
                    w, q = key
                    need(act, "gb", *key)
                    if key == (1, 0):
                        need(act, "pn", 1, 3)
                    copy((g1w, g2w)[w][:, 512 * q:512 * (q + 1)], PS[:, BANK["gb", key], :], kind)
                elif kind == "ysq":
                    t, = key
                    need(act, "mm", ("wo", 3, 3), 1)
                    if t:
                        need(act, "xsq", FFN, 0)
                    act.activation(junk2[:, :].rearrange("p (a b) -> p a b", a=4), PS[:, t:8:2, :], ACT.Square,
                                   accum_out=sums[:, 6 + t:7 + t]).then_inc(S[kind], 1)
                elif kind == "yrt":
                    t, = key
                    need(act, "ysq", t)
                    act.activation(rtmp[:, 6 + t:7 + t], sums[:, 6 + t:7 + t], ACT.Sqrt, bias=cst[:, 0:1],
                                   scale=1.0 / D).then_inc(S[kind], 1)

            def split(slot, land, mm_done):
                act.wait_ge(landed[slot], land)
                act.wait_ge(f_mm, mm_done)
                copy(w_hi[:, slot, :], raw[:, slot, :], "hi")

            def turned_hi(cs, c1):
                act.wait_ge(f_tr, c1)
                for t in range(NT):
                    act.activation(act_hi[:, cs, P * t:P * (t + 1)],
                                   PS[:, 4 + t, :].rearrange("p (a b) -> p a b", a=4), ACT.Copy).then_inc(f_ah, 1)

            def gate_up(c, static):
                for i in range(16):
                    n = R0 + i
                    slot = n % RING
                    if static and c == 0 and i < RING:
                        act.wait_ge(landed[slot], 16 * (n // RING + 1))
                        need(act, "mm", *last_mm(RINGED[R0 - RING + i]))
                        copy(w_hi[:, slot, :], raw[:, slot, :], "hi")
                    else:
                        split(slot, c * 64 + 16 * (n // RING + 1), c * 16 + (i - RING + 1))
                    if i == 9 and not (static and c == 0):
                        turned_hi(slice(4 * (c - 1), 4 * c) if static else ds(c * 4 - 4, 4), c)
                    if i == 11:
                        act.wait_ge(f_mm, c * 16 + 8)
                        if not (static and c == 0):
                            act.wait_ge(f_an, c)
                        act.activation(sgf[:, :, :], PS[:, 0:2, :], ACT.Silu).then_inc(f_sg, 1)

            gate_up(0, True)
            gate_up(1, True)
            with act.Fori(2, FC) as c:
                gate_up(c, False)
            for v in range(ND):
                n = R0 + NG + v
                split(n % RING, 16 * (n // RING + 1), NG + v - RING + 1)
                if v == 4:
                    turned_hi(slice(4 * (FC - 1), 4 * FC), FC)
                if v % 22 == 8 and v > 22:
                    squares(v // 22 - 1) if False else None
                if v in (30, 52, 74):
                    cc = v // 22 - 1
                    act.wait_ge(f_mm, NG + 22 * (cc + 1))
                    for t in range(NT):
                        act.activation(sgf[:, t, :], PS[:, 2 * cc + t, :], ACT.Square,
                                       accum_out=sums[:, 8 + 4 * t + cc:9 + 4 * t + cc]).then_inc(f_sq, 1)
            act.wait_ge(f_mm, NG + ND)
            for t in range(NT):
                act.activation(sgf[:, t, :], PS[:, 6 + t, :], ACT.Square,
                               accum_out=sums[:, 11 + 4 * t:12 + 4 * t]).then_inc(f_sq, 1)
            act.wait_ge(f_rc, 1)
            act.activation(rtmp[:, 0:2], rtmp[:, 2:4], ACT.Sqrt, bias=cst[:, 0:1], scale=1.0 / D).then_inc(f_rt, 1)

        @block.vector
        def _(dve):
            n_chain = [0]

            def step(ins, lag=0):
                n_chain[0] += 1
                ins.then_inc(ch_dve, 1)
                if n_chain[0] > lag:
                    dve.wait_ge(ch_dve, n_chain[0] - lag)

            def four(ap):
                return ap.rearrange("p (a b) -> p a b", a=4)

            for kind, key in PLAN:
                done = S[kind]
                if kind == "lvl":
                    need(dve, "masks")
                    xr = ix[:, 0, :]
                    step(dve.tensor_tensor(xr, ix[:, 0, :], ix[:, 1, :], ALU.bitwise_xor))
                    step(dve.tensor_copy(lt[:, :], xr))
                    for l in range(LEVELS):
                        step(dve.tensor_scalar(lvl[:, l, :], lt[:, :], float(2 ** l), None, ALU.is_ge))
                        ins = dve.scalar_tensor_tensor(out=lvl[:, l, :], in0=lt[:, :], scalar=float(2 ** (l + 1)),
                                                       in1=lvl[:, l, :], op0=ALU.is_lt, op1=ALU.mult)
                    ins.then_inc(done, 1)
                elif kind == "cst":
                    dve.memset(cst[:, 0:1], EPS)
                    dve.memset(cst[:, 1:2], EPS * P)
                    dve.memset(cst[:, 2:3], 1.0)
                    dve.tensor_copy(id_r[:, :], ident[:, :])
                    dve.tensor_scalar(nid_r[:, :], ident[:, :], -1.0, None, ALU.mult).then_inc(done, 1)
                elif kind == "c4l":
                    need(dve, "c4h")
                    dve.tensor_tensor(c4[:, :, 2:4].rearrange("p j w -> p w j"), csil[:, :, :],
                                      c4[:, :, 0:2].bitcast(F32).rearrange("p j w -> p w j"),
                                      ALU.subtract).then_inc(done, 1)
                elif kind == "lo":
                    u, = key
                    need(dve, "hi", u)
                    sz = unit_size(u)
                    hi, lo = wide(u, sz)
                    dve.tensor_tensor(lo, raw[:, at_ring[u] % RING, 0:sz], hi.bitcast(F32),
                                      ALU.subtract).then_inc(done, 1)
                elif kind == "xrc":
                    s, = key
                    need(dve, "xrt", s)
                    dve.reciprocal(rstd[:, 2 * s:2 * s + 2], rtmp[:, 2 * s:2 * s + 2]).then_inc(done, 1)
                elif kind == "xnv":
                    t, = key
                    need(dve, "xrc", FFN)
                    dve.tensor_scalar(xn2[:, t, :], x1[:, t, :], rstd[:, 4 + t:5 + t], None, ALU.mult).then_inc(done, 1)
                elif kind == "s1":
                    need(dve, "modcol")
                    ps = PS[:, BANK["modcol", ()], 0:64].rearrange("p (a b) -> p a b", b=2)
                    dve.tensor_copy(sh1[:, :, :], ps[:, 0:KT, :])
                    dve.scalar_tensor_tensor(out=sc1[:, :, :], in0=ps[:, KT:2 * KT, :], scalar=1.0,
                                             in1=bc(vcol[:, VC_PRE1:VC_PRE1 + KT], 2, 2), op0=ALU.add,
                                             op1=ALU.mult).then_inc(done, 1)
                elif kind == "s2":
                    need(dve, "mcc", 15)
                    dve.scalar_tensor_tensor(out=sc2[:, :], in0=modc[:, 2 * KT:3 * KT], scalar=1.0,
                                             in1=vcol[:, VC_PRE2:VC_PRE2 + KT], op0=ALU.add,
                                             op1=ALU.mult).then_inc(done, 1)
                elif kind == "hf":
                    s, kp = key
                    need(dve, "xT", s, kp)
                    if kp >= 2:
                        need(dve, "hhi", s, kp - 2)
                        need(dve, "hlo", s, kp - 2)
                    elif s == LAT:
                        need(dve, "hhi", CTX, kp + 6)
                        need(dve, "hlo", CTX, kp + 6)
                    buf = hf2 if s == FFN else hfs
                    need(dve, "s2" if s == FFN else "s1")
                    for k in range(2):
                        kt = 2 * kp + k
                        scale = sc2[:, kt:kt + 1] if s == FFN else sc1[:, kt, s:s + 1]
                        shift = modc[:, KT + kt:KT + kt + 1] if s == FFN else sh1[:, kt, s:s + 1]
                        ins = dve.tensor_scalar(buf[:, kp % 2, k, :], PS[:, BANK["xT", key], T * k:T * (k + 1)],
                                                scale, shift, ALU.mult, ALU.add)
                    ins.then_inc(done, 1)
                elif kind == "hlo":
                    s, kp = key
                    need(dve, "hhi", s, kp)
                    buf = hf2 if s == FFN else hfs
                    hi, lo = seq_h[s]
                    dve.tensor_tensor(lo[:, 2 * kp:2 * kp + 2, :], buf[:, kp % 2, :, :],
                                      hi[:, 2 * kp:2 * kp + 2, :].bitcast(F32), ALU.subtract).then_inc(done, 1)
                elif kind == "ny":
                    s, = key
                    pr = projection(dve, ("ba", s))[:, 0:64].rearrange("p (t n) -> p t n", t=NT)
                    g = gates_[s]
                    need(dve, "bsig", s)
                    dve.wait_ge(small_in["dt"], 32)
                    for d in range(2):
                        ins = dve.tensor_tensor(g["y0"][:, d, :, :], pr[:, :, 16 + 8 * d:24 + 8 * d],
                                                bc(dtb[:, 8 * d:8 * d + 8], 1, NT), ALU.add)
                    step(ins)
                    step(dve.tensor_scalar(g["y1"][:, :, :, :], g["y0"][:, :, :, :], 0.0, None, ALU.max))
                    dve.scalar_tensor_tensor(out=g["y2"][:, :, :, :], in0=g["y1"][:, :, :, :], scalar=-2.0,
                                             in1=g["y0"][:, :, :, :], op0=ALU.mult, op1=ALU.add).then_inc(done, 1)
                elif kind == "gg":
                    s, = key
                    g = gates_[s]
                    need(dve, "nln", s)
                    need(dve, "ny", s)
                    need(dve, "nega")
                    step(dve.tensor_tensor(g["y0"][:, :, :, :], g["y1"][:, :, :, :], g["y2"][:, :, :, :], ALU.add))
                    for d in range(2):
                        ins = dve.scalar_tensor_tensor(out=g["g"][:, d, :, :], in0=g["y0"][:, d, :, :], scalar=-1.0,
                                                       in1=bc(nega[:, 8 * d:8 * d + 8], 1, NT), op0=ALU.mult,
                                                       op1=ALU.mult)
                    ins.then_inc(done, 1)
                elif kind == "nbe":
                    s, = key
                    g = gates_[s]
                    need(dve, "bsig", s)
                    need(dve, "eall", s)
                    step(dve.tensor_scalar(g["nbeta"][:, :, :, :], g["beta"][:, :, :, :], -1.0, None, ALU.mult))
                    dve.tensor_tensor(g["y0"][:, :, :, :], g["nbeta"][:, :, :, :], ex[s][:, 0, :, :, :],
                                      ALU.mult).then_inc(done, 1)
                elif kind == "taps":
                    n = conv_cus.index(key)
                    what, s, p = key
                    need(dve, "tap2", *key)
                    pr = projection(dve, key)
                    for tap in (0, 1, 3, 4):
                        off = tap - W5 // 2
                        a, b = max(0, -off), T - max(0, off)
                        for h in range(2):
                            col = VC_C5 + tap * 24 + CU_TILE[what] + 2 * p + h
                            o = sil[:, n % 2, h, a:b]
                            ins = dve.scalar_tensor_tensor(out=o, in0=pr[:, T * h + a + off:T * h + b + off],
                                                           scalar=vcol[:, col:col + 1], in1=o, op0=ALU.mult,
                                                           op1=ALU.add)
                            if (tap, h) != (4, 1):
                                step(ins, 1)
                    ins.then_inc(done, 1)
                elif kind == "nsq":
                    s, what, p = key
                    need(dve, "natc", what, s, p)
                    before = PAIRS[PAIRS.index((s, p)) - 1]
                    if what == "q":
                        need(dve, "nsq", s, "k", p)
                    elif (s, p) == PAIRS[0]:
                        need(dve, "hlo", LAT, 7)
                    elif before[0] == CTX:
                        need(dve, "st", *before, 1)
                    else:
                        need(dve, "mix_hi", before[1])
                        need(dve, "mix_lo", before[1])
                    a = 8 if what == "k" else 12
                    kq = kvq[what][:, PAIRS.index((s, p)) % 2, :, :, :].rearrange("p t h d -> p (t h) d")
                    step(dve.tensor_tensor(four(tmp), kq, kq, ALU.mult))
                    dve.tensor_reduce(sums[:, a:a + 4], four(tmp), AX_X, ALU.add).then_inc(done, 1)
                elif kind == "nrc":
                    need(dve, "nrt", *key)
                    a = 8 if key[1] == "k" else 12
                    dve.reciprocal(rstd[:, a:a + 4], rtmp[:, a:a + 4]).then_inc(done, 1)
                elif kind == "kn":
                    s, what, p = key
                    need(dve, "nrc", *key)
                    a = 8 if what == "k" else 12
                    kq = kvq[what][:, PAIRS.index((s, p)) % 2, :, :, :].rearrange("p t h d -> p (t h) d")
                    dve.tensor_tensor(kq, kq, bc(rstd[:, a:a + 4], 2, P), ALU.mult).then_inc(done, 1)
                elif kind == "gk":
                    s, p, t = key
                    n = 4 if s == LAT else 2
                    need(dve, "kk", *key)
                    need(dve, "edec", *key)
                    e = e_[:, 0:n, :].rearrange("p a b -> p (a b)")
                    dve.tensor_tensor(e, PS[:, BANK["kk", key], 0:n * P], e, ALU.mult).then_inc(done, 1)
                elif kind == "mneg":
                    s, p, t = key
                    need(dve, "gk", *key)
                    need(dve, "nbe", s)
                    k = PAIRS.index((s, p))
                    if k:
                        need(dve, "vn", *PAIRS[k - 1], 1)
                    for d, m in enumerate((m_gt, m_lt)):
                        for h in range(2):
                            ins = dve.scalar_tensor_tensor(
                                out=mn[:, t, 2 * d + h, :], in0=e_[:, h, :],
                                scalar=gates_[s]["nbeta"][:, d, t, 2 * p + h:2 * p + h + 1], in1=m[:, :],
                                op0=ALU.mult, op1=ALU.mult)
                    ins.then_inc(done, 1)
                elif kind in ("xadd", "yadd"):
                    s, p, t, l = key
                    buf = (xi if kind == "xadd" else yi)[:, t, :, :]
                    if l == 0:
                        need(dve, "z", *key)
                        k = PAIRS.index((s, p))
                        if k:
                            need(dve, "nx", *PAIRS[k - 1], t)
                        if kind == "xadd":
                            a = four(PS[:, BANK["z", key], :])
                        else:
                            a = mkl[:, t, :, :].bitcast(F32)
                        dve.tensor_tensor(buf, a, bc(ident[:, :], 1, 4), ALU.add).then_inc(done, 1)
                    else:
                        need(dve, "xy", *key)
                        dve.wait_ge(done, COUNT[kind, (s, p, t, l - 1)])
                        a = four(PS[:, BANK["xy", key, kind[0]], :])
                        dve.tensor_tensor(buf, a, buf.bitcast(F32), ALU.add).then_inc(done, 1)
                elif kind == "nrr":
                    t = key[2]
                    need(dve, "nr", *key)
                    dve.tensor_tensor(zi[:, t, :, :], four(PS[:, BANK["nr", key], :]), bc(ident[:, :], 1, 4),
                                      ALU.add).then_inc(done, 1)
                elif kind == "xf":
                    t = key[2]
                    need(dve, "nx", *key)
                    dve.tensor_tensor(mn[:, t, :, :], four(PS[:, BANK["nx", key], :]), xi[:, t, :, :].bitcast(F32),
                                      ALU.add).then_inc(done, 1)
                elif kind == "r":
                    s, p, i = key
                    need(dve, "ks", *key)
                    need(dve, "vb", *key)
                    for d in range(2):
                        for h in range(2):
                            n = 2 * d + h
                            ins = dve.scalar_tensor_tensor(
                                out=rb[:, n, :], in0=PS[:, BANK["ks", key], P * n:P * (n + 1)],
                                scalar=gates_[s]["y0"][:, d, tile_of(d, i), 2 * p + h:2 * p + h + 1],
                                in1=rb[:, n, :], op0=ALU.mult, op1=ALU.add)
                    ins.then_inc(done, 1)
                elif kind == "stc":
                    s, p, i = key
                    need(dve, "st", *key)
                    ps = PS[:, BANK["st", key], :]
                    if s == CTX and i == 0:
                        dve.tensor_copy(sctx[:, p, :, :], four(ps)).then_inc(done, 1)
                        continue
                    if s == CTX:
                        need(dve, "stc", s, p, 0)
                    elif p:
                        need(dve, "o", p - 1)
                    new = sctx[:, p, :, :] if s == CTX else slat[:, :, :]
                    for d in range(2):
                        for h in range(2):
                            n = 2 * d + h
                            ins = dve.scalar_tensor_tensor(
                                out=new[:, n, :], in0=sctx[:, p, n, :],
                                scalar=ex[s][:, 2, d, tile_of(d, i), 2 * p + h:2 * p + h + 1],
                                in1=ps[:, P * n:P * (n + 1)], op0=ALU.mult, op1=ALU.add)
                    ins.then_inc(done, 1)
                elif kind == "osq":
                    need(dve, "oc", *key)
                    step(dve.tensor_tensor(four(tmp), rb[:, :, :], rb[:, :, :], ALU.mult))
                    dve.tensor_reduce(sums[:, 8:12], four(tmp), AX_X, ALU.add).then_inc(done, 1)
                elif kind == "orc":
                    need(dve, "ort", *key)
                    dve.reciprocal(rstd[:, 8:12], rtmp[:, 8:12]).then_inc(done, 1)
                elif kind == "on":
                    need(dve, "orc", *key)
                    dve.tensor_tensor(rb[:, :, :], rb[:, :, :], bc(rstd[:, 8:12], 2, P), ALU.mult).then_inc(done, 1)
                elif kind == "ym":
                    p, = key
                    need(dve, "oT", p)
                    need(dve, "zsilu", "z", LAT, p)
                    ps = PS[:, BANK["oT", key], :].rearrange("p (t h c) -> p t h c", t=NT, h=2)
                    y = kd[:, :, :].rearrange("p (h t) c -> p h t c", h=2)
                    for h in range(2):
                        ins = dve.scalar_tensor_tensor(
                            out=y[:, h, :, :], in0=ps[:, :, h, :], scalar=vcol[:, VC_ON:VC_ON + 1],
                            in1=zs[:, p % 2, h, :].rearrange("p (t c) -> p t c", t=NT), op0=ALU.mult, op1=ALU.mult)
                    ins.then_inc(done, 1)
                elif kind == "mix_lo":
                    n, = key
                    need(dve, "mix_hi", n)
                    src = kd[:, :, :].rearrange("p a b -> p (a b)") if n < NP else ub[:, :]
                    dve.tensor_tensor(hc_lo[:, 2 * n:2 * n + 2, :].rearrange("p a b -> p (a b)"), src,
                                      hc_hi[:, 2 * n:2 * n + 2, :].bitcast(F32).rearrange("p a b -> p (a b)"),
                                      ALU.subtract).then_inc(done, 1)
                elif kind == "u":
                    i, = key
                    need(dve, "sg", i)
                    if i:
                        need(dve, "dw", i - 1, 5)
                    dve.tensor_tensor(ub[:, :], projection(dve, ("a", LAT, i)), sgb[:, :], ALU.mult).then_inc(done, 1)
                elif kind == "dw":
                    i, n = key
                    taps = [k for k in range(W31) if k != W31 // 2][5 * n:5 * n + 5]
                    if n == 0:
                        need(dve, "u", i)
                        taps = [W31 // 2] + taps
                    else:
                        need(dve, "dw", i, n - 1)
                    for tap in taps:
                        off = tap - W31 // 2
                        a, b = max(0, -off), ROW - max(0, off)
                        for h in range(2):
                            col = VC_C31 + tap * 8 + 2 * i + h
                            src = ub[:, T * h:T * (h + 1)].rearrange("p (r w) -> p r w", w=ROW)[:, :, a + off:b + off]
                            dst = cacc[:, 2 * i + h, :].rearrange("p (r w) -> p r w", w=ROW)[:, :, a:b]
                            if off == 0:
                                ins = dve.tensor_scalar(dst, src, vcol[:, col:col + 1], None, ALU.mult)
                            else:
                                ins = dve.scalar_tensor_tensor(out=dst, in0=src, scalar=vcol[:, col:col + 1],
                                                               in1=dst, op0=ALU.mult, op1=ALU.add)
                            if (tap, h) != (taps[-1], 1):
                                step(ins, 1)
                    ins.then_inc(done, 1)
                elif kind == "cen":
                    need(dve, "lnm")
                    dve.scalar_tensor_tensor(out=cacc[:, :, :], in0=bc(PS[:, BANK["lnm", ()], 0:T], 1, 8),
                                             scalar=-1.0 / DC, in1=cacc[:, :, :], op0=ALU.mult,
                                             op1=ALU.add).then_inc(done, 1)
                elif kind == "lva":
                    i, = key
                    need(dve, "lnv", i)
                    ps = PS[:, BANK["lnv", key], 0:T]
                    if i == 0:
                        dve.tensor_copy(cx[:, 0, :], ps).then_inc(done, 1)
                    else:
                        need(dve, "lva", i - 1)
                        dve.tensor_tensor(cx[:, 0, :], ps, cx[:, 0, :], ALU.add).then_inc(done, 1)
                elif kind == "lnr":
                    need(dve, "lsd")
                    dve.reciprocal(cx[:, 0, :], cx[:, 1, :]).then_inc(done, 1)
                elif kind == "lnn":
                    need(dve, "lnr")
                    dve.tensor_tensor(cacc[:, :, :], cacc[:, :, :], bc(cx[:, 0, :], 1, 8), ALU.mult).then_inc(done, 1)
                elif kind == "macc":
                    m, j = key
                    n = at_ring["mr", m, j]
                    dve.wait_ge(landed[n % RING], 16 * (n // RING + 1))
                    if j == 0:
                        need(dve, "csil")
                        if m:
                            need(dve, "mcol", m - 1)
                        step(dve.tensor_scalar(macc[:, :], raw[:, n % RING, 0:512], csil[:, LAT, 0:1], None, ALU.mult))
                    else:
                        need(dve, "macc", m, j - 1)
                        step(dve.scalar_tensor_tensor(out=macc[:, :], in0=raw[:, n % RING, 0:512],
                                                      scalar=csil[:, LAT, 2 * j:2 * j + 1], in1=macc[:, :],
                                                      op0=ALU.mult, op1=ALU.add))
                    dve.scalar_tensor_tensor(out=macc[:, :], in0=raw[:, n % RING, 512:1024],
                                             scalar=csil[:, LAT, 2 * j + 1:2 * j + 2], in1=macc[:, :],
                                             op0=ALU.mult, op1=ALU.add).then_inc(done, 1)
                elif kind == "mcc":
                    m, = key
                    need(dve, "mcol", m)
                    dve.tensor_tensor(modc[:, 4 * m:4 * m + 4], PS[:, BANK["mcol", key], 0:4],
                                      vcol[:, VC_MOD + 4 * m:VC_MOD + 4 * m + 4], ALU.add).then_inc(done, 1)
                elif kind == "gdiag":
                    w, q = key
                    need(dve, "mcc", 15)
                    need(dve, "mix_lo", NP - 1)
                    if (w, q) != (0, 0):
                        need(dve, "gb", *((w, q - 1) if q else (0, 3)))
                    for i in range(4):
                        g = (0, 3 * KT)[w] + 4 * q + i
                        v = (VC_POST1, VC_POST2)[w] + 4 * q + i
                        ins = dve.tensor_scalar(sgf[:, 0, P * i:P * (i + 1)], ident[:, :], modc[:, g:g + 1],
                                                vcol[:, v:v + 1], ALU.mult, ALU.mult)
                    ins.then_inc(done, 1)
                elif kind == "yrc":
                    t, = key
                    need(dve, "yrt", t)
                    dve.reciprocal(rstd[:, 6 + t:7 + t], rtmp[:, 6 + t:7 + t]).then_inc(done, 1)
                elif kind == "pn":
                    t, cc = key
                    need(dve, "yrc", t)
                    need(dve, "gbc", 0, 3)
                    if COUNT[kind, key] > 2:
                        dve.wait_ge(S["pa"], COUNT[kind, key] - 2)
                    dve.scalar_tensor_tensor(out=anf[:, cc % 2, :], in0=PS[:, 2 * cc + t, :],
                                             scalar=rstd[:, 6 + t:7 + t], in1=g1w[:, 512 * cc:512 * (cc + 1)],
                                             op0=ALU.mult, op1=ALU.mult).then_inc(done, 1)

            def split(slot, count):
                dve.wait_ge(S["hi"], count)
                dve.tensor_tensor(w_lo[:, slot, :], raw[:, slot, :], w_hi[:, slot, :].bitcast(F32),
                                  ALU.subtract).then_inc(S["lo"], 1)

            def product(c, static):
                dve.wait_ge(f_mm, c * 16)
                dve.wait_ge(f_sg, c)
                if not (static and c < 2):
                    dve.wait_ge(f_tr, c - 1)
                dve.tensor_tensor(anf[:, :, :], PS[:, 2:4, :], sgf[:, :, :], ALU.mult).then_inc(f_an, 1)

            def turned_lo(cs, c1, ah):
                dve.wait_ge(f_ah, ah)
                for t in range(NT):
                    dve.tensor_tensor(act_lo[:, cs, P * t:P * (t + 1)], four(PS[:, 4 + t, :]),
                                      act_hi[:, cs, P * t:P * (t + 1)].bitcast(F32), ALU.subtract).then_inc(f_al, 1)

            def gate_up(c, static):
                for i in range(16):
                    split((R0 + i) % RING, c * 16 + (B0 + i + 1))
                    if static and c == 0:
                        continue
                    if i == 3:
                        product(c, static)
                    if i == 9:
                        turned_lo(slice(4 * (c - 1), 4 * c) if static else ds(c * 4 - 4, 4), c, c * 2)

            gate_up(0, True)
            gate_up(1, True)
            with dve.Fori(2, FC) as c:
                gate_up(c, False)
            for v in range(ND):
                split((R0 + NG + v) % RING, B0 + NG + v + 1)
                if v == 1:
                    product(FC, True)
                if v == 4:
                    turned_lo(slice(4 * (FC - 1), 4 * FC), FC, 2 * FC)
                if v in (30, 52, 74):
                    cc = v // 22 - 1
                    dve.wait_ge(f_sq, 2 * cc + 2)
                    for t in range(NT):
                        b = PS[:, 2 * cc + t, :]
                        dve.tensor_tensor(b, b, g2w[:, 512 * cc:512 * (cc + 1)], ALU.mult).then_inc(f_yg, 1)
            dve.wait_ge(f_sq, 8)
            dve.tensor_reduce(rtmp[:, 2:4], sums[:, 8:16].rearrange("p (t c) -> p t c", t=NT), AX_X,
                              ALU.add).then_inc(f_rc, 1)
            for t in range(NT):
                b = PS[:, 6 + t, :]
                dve.tensor_tensor(b, b, g2w[:, 1536:2048], ALU.mult).then_inc(f_yg, 1)
            dve.wait_ge(f_rt, 1)
            step(dve.reciprocal(rstd[:, 0:2], rtmp[:, 0:2]))
            dve.wait_ge(f_yg, 8)
            for t in range(NT):
                for cc in range(4):
                    xc = x1[:, t, 512 * cc:512 * (cc + 1)]
                    dve.scalar_tensor_tensor(out=xc, in0=PS[:, 2 * cc + t, :], scalar=rstd[:, t:t + 1], in1=xc,
                                             op0=ALU.mult, op1=ALU.add).then_inc(f_out, 1)

        @block.tensor
        def _(pe):
            def product(out_ap, a, b, cols, start, stop, grouped=False):
                for n, (i, j) in enumerate(((0, 0), (0, 1), (1, 0))):
                    ins = pe.matmul(out_ap, a[i], b[j], start=start and n == 0, stop=stop and n == 2,
                                    skip_group_check=grouped)
                return ins

            def turn4(bank_, srcs):
                for n, src in enumerate(srcs):
                    ins = pe.transpose(PS[:, bank_, P * n:P * (n + 1)], src, ident[:, :])
                return ins

            for kind, key in PLAN:
                done = S[kind] if kind in S else None
                if kind == "vT":
                    n, = key
                    need(pe, "masks")
                    pe.wait_ge(small_in["vec"], 16 * 11)
                    b = aux(pe, kind, key)
                    for v, rows, col in (((0, 81, 0), (1, 64, 128), (2, 120, 256)), ((3, 124, 0), (4, 124, 124)))[n]:
                        ins = pe.transpose(PS[:, b, col:col + rows], vnat[0:rows, v, :], ident[0:rows, 0:rows])
                    ins.then_inc(done, 1)
                elif kind == "mm":
                    u, half = key
                    if half == 0:
                        need(pe, "hi", u)
                        need(pe, "lo", u)
                    hi, lo = wide(u, unit_size(u))
                    if u[0] == "mod":
                        _, hf, j, q = u
                        if (hf, j, q) == (0, 0, 0):
                            need(pe, "c4l")
                        if (hf, j, q) == (1, 0, 0):
                            need(pe, "mrow", 0)
                        for n in range(2):
                            for m, w in enumerate((hi, lo)):
                                ins = pe.matmul(PS[0:4, 2 * q + n, :], c4[:, j, :], w[:, 512 * n:512 * (n + 1)],
                                                start=j == 0 and m == 0, stop=j == KT - 1 and m == 1)
                    elif u[0] == "ba":
                        s = u[1]
                        b = proj_bank[u]
                        need(pe, "mrow", 1)
                        need(pe, "hlo", s, 7)
                        for r in ([] if projected.index(u) < 4 else first_read(projected[projected.index(u) - 4])):
                            need(pe, r[0], *r[1])
                        hh, hl = seq_h[s]
                        for t in range(NT):
                            for kt in range(KT):
                                tok, col = slice(P * t, P * (t + 1)), slice(32 * kt, 32 * kt + 32)
                                ins = product(PS[:, b, 32 * t:32 * t + 32], (hh[:, kt, tok], hl[:, kt, tok]),
                                              (hi[:, col], lo[:, col]), 32, kt == 0, kt == KT - 1)
                    elif u[0] == "win":
                        cu, g = u[1:]
                        s = cu[1]
                        b = proj_bank[cu]
                        if (g, half) == (0, 0):
                            k = projected.index(cu)
                            for r in first_read(projected[k - 4]) if k >= 4 else []:
                                need(pe, r[0], *r[1])
                            need(pe, "mrow", 1)
                            need(pe, "hlo", s, 7)
                        hh, hl = seq_h[s]
                        for k in range(2):
                            kt = 4 * g + 2 * half + k
                            for h in range(2):
                                col = slice(256 * (2 * half + k) + P * h, 256 * (2 * half + k) + P * (h + 1))
                                ins = product(PS[:, b, T * h:T * (h + 1)], (hi[:, col], lo[:, col]),
                                              (hh[:, kt, :], hl[:, kt, :]), T, kt == 0 and h == 0, kt == KT - 1, True)
                    else:
                        _, cc, kg = u
                        kt = 2 * kg + half
                        need(pe, "mix_lo", NP + (kt - 8) // 2 if kt >= 8 else kt // 2)
                        if (kg, half) == (4, 0):
                            if cc < 2:
                                for w in projected[-4:]:
                                    for r in first_read(w):
                                        need(pe, r[0], *r[1])
                            else:
                                need(pe, "gbc", 0, 3)
                        for t in range(NT):
                            tok, col = slice(P * t, P * (t + 1)), slice(512 * half, 512 * (half + 1))
                            ins = product(PS[:, 2 * cc + t, :], (hc_hi[:, kt, tok], hc_lo[:, kt, tok]),
                                          (hi[:, col], lo[:, col]), 512, (kg, half) == (4, 0), (kg, half) == (3, 1))
                    ins.then_inc(done, 1)
                elif kind == "modcol":
                    need(pe, "mrow", 1)
                    pe.wait_ge(small_in["bmod"], 16)
                    b = aux(pe, kind, key)
                    need(pe, "xsq", 1, 1)
                    for n in range(2 * KT):
                        ins = pe.matmul(PS[:, b, 2 * n:2 * n + 2], modrow[0:5, P * n:P * (n + 1)], sel[0:5, :],
                                        start=True, stop=True)
                    ins.then_inc(done, 1)
                elif kind == "xT":
                    s, kp = key
                    b = aux(pe, kind, key)
                    if s == FFN:
                        need(pe, "xnv", 1)
                        need(pe, "pn", 1, 3)
                        src = xn2
                    else:
                        need(pe, "xn", s, 1)
                        src = xs[s]
                    turn4(b, [src[:, t, P * (2 * kp + k):P * (2 * kp + k + 1)] for k in range(2) for t in range(NT)])\
                        .then_inc(done, 1)
                elif kind == "pref":
                    s, = key
                    need(pe, "gg", s)
                    b = aux(pe, kind, key)
                    for k, ms in enumerate(((m_le, m_ge), (m_gt, m_lt), (ones, ones))):
                        for d in range(2):
                            ins = pe.matmul(PS[:, b, 16 * (2 * k + d):16 * (2 * k + d + 1)], ms[d][:, :],
                                            gates_[s]["g"][:, d, :, :].rearrange("p t h -> p (t h)"),
                                            start=True, stop=True)
                    ins.then_inc(done, 1)
                elif kind == "nat":
                    n = conv_cus.index(key)
                    need(pe, "csilu", *key)
                    b = aux(pe, kind, key)
                    turn4(b, [sil[:, n % 2, h, P * t:P * (t + 1)] for t in range(NT) for h in range(2)])\
                        .then_inc(done, 1)
                elif kind in ("kT", "qT"):
                    if kind == "kT":
                        s, p = key
                        need(pe, "kn", s, "k", p)
                        src = kvq["k"][:, PAIRS.index((s, p)) % 2, :, :, :]
                    else:
                        p, k = key
                        need(pe, "kn", LAT, "q", p)
                        if k:
                            need(pe, "qdec", p, k)
                        src = qx[:, :, :, :] if k else kvq["q"][:, PAIRS.index((LAT, p)) % 2, :, :, :]
                    b = aux(pe, kind, key)
                    turn4(b, [src[:, t, h, :] for t in range(NT) for h in range(2)]).then_inc(done, 1)
                elif kind == "dec":
                    s, p, t, k = key
                    need(pe, "gm", *key)
                    b = BANK["dec", (s, p, t, 0)] if k else aux(pe, kind, key)
                    for d, m in enumerate(((m_le, m_ge), (m_gt, m_lt))[k]):
                        ins = pe.matmul(PS[:, b, T * k:T * (k + 1)], m[:, :],
                                        gmv[:, d, :, :].rearrange("p h c -> p (h c)"), start=d == 0, stop=d == 1)
                    ins.then_inc(done, 1)
                elif kind == "kk":
                    s, p, t = key
                    need(pe, "kTc", s, p)
                    if s == LAT:
                        need(pe, "qTc", p, 0)
                    b = aux(pe, kind, key)
                    for n in range(4 if s == LAT else 2):
                        rhs = kTs[:, t, n, :] if n < 2 else qTs[:, 0, t, n - 2, :]
                        ins = pe.matmul(PS[:, b, P * n:P * (n + 1)], kTs[:, t, n % 2, :], rhs, start=True, stop=True)
                    ins.then_inc(done, 1)
                elif kind == "z":
                    s, p, t, l = key
                    need(pe, "mk", *key)
                    if l:
                        need(pe, "xadd", s, p, t, l - 1)
                    else:
                        need(pe, "cst")
                    b = aux(pe, kind, key)
                    for n in range(4):
                        ins = pe.matmul(PS[:, b, P * n:P * (n + 1)], mkl[:, t, n, :],
                                        xi[:, t, n, :] if l else id_r[:, :], start=True, stop=True)
                    ins.then_inc(done, 1)
                elif kind == "xy":
                    s, p, t, l = key
                    need(pe, "zc", *key)
                    need(pe, "yadd", s, p, t, l - 1)
                    bx, by = aux(pe, kind, key, "x"), aux(pe, kind, key, "y")
                    for n in range(4):
                        pe.matmul(PS[:, bx, P * n:P * (n + 1)], yi[:, t, n, :], zi[:, t, n, :], start=True, stop=True)
                    for n in range(4):
                        ins = pe.matmul(PS[:, by, P * n:P * (n + 1)], zi[:, t, n, :], yi[:, t, n, :],
                                        start=True, stop=True)
                    ins.then_inc(done, 1)
                elif kind == "nr":
                    s, p, t = key
                    need(pe, "mlo", *key)
                    need(pe, "xadd", s, p, t, LEVELS - 1)
                    b = aux(pe, kind, key)
                    for n in range(4):
                        for k, w in enumerate((mhi[:, t, n, :], mkl[:, t, n, :], nid_r[:, :])):
                            ins = pe.matmul(PS[:, b, P * n:P * (n + 1)], w, xi[:, t, n, :], start=k == 0, stop=k == 2)
                    ins.then_inc(done, 1)
                elif kind == "nx":
                    s, p, t = key
                    need(pe, "nrr", *key)
                    need(pe, "yadd", s, p, t, LEVELS - 1)
                    b = aux(pe, kind, key)
                    for n in range(4):
                        ins = pe.matmul(PS[:, b, P * n:P * (n + 1)], yi[:, t, n, :], zi[:, t, n, :],
                                        start=True, stop=True)
                    ins.then_inc(done, 1)
                elif kind in ("ks", "vn", "st"):
                    s, p, i = key
                    if kind == "ks":
                        need(pe, "kTc", s, p)
                        need(pe, "stc", *((s, p, 0) if i else (CTX, p, 1)))
                        state = slat if (s, i) == (LAT, 1) else sctx[:, p, :, :]
                    elif kind == "vn":
                        need(pe, "xf", s, p, 1)
                        need(pe, "vb", *key)
                        if (kind := "vn") and ("r", key) in COUNT:
                            need(pe, "r", *key)
                    else:
                        need(pe, "kd", *key)
                        need(pe, "vnc", *key)
                    b = aux(pe, kind, key)
                    for d in range(2):
                        for h in range(2):
                            n, t = 2 * d + h, tile_of(d, i)
                            if kind == "ks":
                                a, m = kTs[:, t, h, :], state[:, n, :]
                            elif kind == "vn":
                                a, m = mn[:, t, n, :], rb[:, n, :]
                            else:
                                a, m = kd[:, n, :], vnew[:, i, n, :]
                            ins = pe.matmul(PS[:, b, P * n:P * (n + 1)], a, m, start=True, stop=True)
                    ins.then_inc(done, 1)
                elif kind == "o":
                    p, = key
                    need(pe, "qTc", p, 2)
                    need(pe, "vnc", LAT, p, 1)
                    need(pe, "attn", p, 1)
                    b = aux(pe, kind, key)
                    for t in range(NT):
                        for h in range(2):
                            for d in range(2):
                                i = tile_of(d, t)
                                state = slat if i else sctx[:, p, :, :]
                                o = PS[:, b, P * (2 * t + h):P * (2 * t + h + 1)]
                                pe.matmul(o, qTs[:, 1 + d, t, h, :], state[:, 2 * d + h, :], start=d == 0, stop=False)
                                ins = pe.matmul(o, at[:, t, d, h, :], vnew[:, i, 2 * d + h, :], start=False,
                                                stop=d == 1)
                    ins.then_inc(done, 1)
                elif kind == "oT":
                    need(pe, "on", *key)
                    b = aux(pe, kind, key)
                    turn4(b, [rb[:, n, :] for n in range(4)]).then_inc(done, 1)
                elif kind == "lnm":
                    need(pe, "dw", 3, 5)
                    b = aux(pe, kind, key)
                    for n in range(8):
                        ins = pe.matmul(PS[:, b, 0:T], ones[:, :], cacc[:, n, :], start=n == 0, stop=n == 7)
                    ins.then_inc(done, 1)
                elif kind == "lnv":
                    need(pe, "csq", *key)
                    b = aux(pe, kind, key)
                    for n in range(2):
                        ins = pe.matmul(PS[:, b, 0:T], ones[:, :], ub[:, T * n:T * (n + 1)], start=n == 0, stop=n == 1)
                    ins.then_inc(done, 1)
                elif kind == "mcol":
                    m, = key
                    need(pe, "macc", m, 7)
                    b = aux(pe, kind, key)
                    for n in range(4):
                        ins = pe.matmul(PS[:, b, n:n + 1], macc[:, P * n:P * (n + 1)], ones[:, 0:1],
                                        start=True, stop=True)
                    ins.then_inc(done, 1)
                elif kind == "gb":
                    need(pe, "gdiag", *key)
                    b = aux(pe, kind, key)
                    pe.matmul(PS[:, b, :], ones[:, :], sgf[:, 0, :], start=True, stop=True).then_inc(done, 1)

            def unit(slot, ready, k0, left, banks, first, last):
                pe.wait_ge(S["hi"], ready)
                pe.wait_ge(S["lo"], ready)
                for k in range(2):
                    col = slice(512 * k, 512 * (k + 1))
                    for t in range(NT):
                        tok = slice(P * t, P * (t + 1))
                        ins = product(PS[:, banks + t, :], (left[0][:, k0 + k, tok], left[1][:, k0 + k, tok]),
                                      (w_hi[:, slot, col], w_lo[:, slot, col]), 512, first and k == 0, last and k == 1)
                ins.then_inc(f_mm, 1)

            def turn(c, static):
                pe.wait_ge(f_an, c)
                if static and c == 1:
                    need(pe, "gbc", 1, 3)
                else:
                    pe.wait_ge(f_al, c * 2 - 2)
                for t in range(NT):
                    ins = turn4(4 + t, [anf[:, t, P * f:P * (f + 1)] for f in range(4)])
                ins.then_inc(f_tr, 1)

            def gate_up(c, static):
                for i in range(16):
                    if static and c == 0:
                        if i == 0:
                            need(pe, "hlo", FFN, 7)
                            need(pe, "pn", 1, 3)
                    elif i == 0:
                        pe.wait_ge(f_sg, c)
                    elif i == 8:
                        pe.wait_ge(f_an, c)
                    unit((R0 + i) % RING, c * 16 + (B0 + i + 1), 2 * (i % 8), (h_hi, h_lo), 0 if i < 8 else 2,
                         i % 8 == 0, i % 8 == 7)
                    if i == 5 and not (static and c == 0):
                        turn(c, static)

            gate_up(0, True)
            gate_up(1, True)
            with pe.Fori(2, FC) as c:
                gate_up(c, False)
            for v in range(ND):
                cc, g = divmod(v, FT // 2)
                if v == 0:
                    pe.wait_ge(f_sg, FC)
                    pe.wait_ge(f_al, 2 * FC - 2)
                if v == 20:
                    pe.wait_ge(f_al, 2 * FC)
                unit((R0 + NG + v) % RING, B0 + NG + v + 1, 2 * g, (act_hi, act_lo), 2 * cc, g == 0,
                     g == FT // 2 - 1)
                if v == 2:
                    turn(FC, True)


_INS = ["x", "c", "ctx", "c_ctx", "w_mod", "b_mod", "mix_norm_pre", "mix_norm_post", "w_in", "qkv_conv", "a_log",
        "dt_bias", "delta_out_norm", "conf_dw", "conf_ln_w", "conf_ln_b", "w_out", "ffn_norm_pre", "ffn_norm_post",
        "w_gate", "w_up", "w_down"]


def kernel(**inputs):
    import numpy as np
    import concourse.bacc as bacc
    from concourse.bass_utils import run_bass_kernel_spmd

    nc = bacc.Bacc("TRN2", target_bir_lowering=False, num_devices=1)
    arrays, args = {}, []
    for name in _INS:
        a = np.ascontiguousarray(inputs[name])
        arrays[f"in_{name}_dram"] = a
        args.append(nc.dram_tensor(f"in_{name}_dram", a.shape, mybir.dt.from_np(a.dtype), kind="ExternalInput").ap())
    args.append(nc.dram_tensor("out_dram", (1, T, D), F32, kind="ExternalOutput").ap())
    layer(nc, *args)
    return run_bass_kernel_spmd(nc, [arrays], core_ids=[0]).results[0]["out_dram"]
```

```python
from contextlib import ExitStack

import concourse.bass as bass
from concourse import mybir

F32 = mybir.dt.float32
F32R = mybir.dt.float32r
I32 = mybir.dt.int32
ALU = mybir.AluOpType
ACT = mybir.ActivationFunctionType
AX_X = mybir.AxisListType.X
ds = bass.ds

P = 128
D = 2048
KT = D // P
T = 256
NT = T // P
H = 8
NP = H // 2
ROW = 64
W5, W31 = 5, 31
DD = H * P
DC = D - DD
ST_END = 3 * DD + 4 * H
Z_END = ST_END + DD
DFF = 5632
FT = DFF // P
FC = DFF // 512
EPS = 1e-6
RING = 4
AHEAD = 2
UN = 1024
SLACK = 4
NDW = 15
LEVELS = 7
CTX, LAT, FFN = 0, 1, 2

VC_PRE1, VC_PRE2, VC_POST1, VC_POST2, VC_LNW, VC_LNB, VC_ON = 0, 16, 32, 48, 64, 72, 80
VC_MOD = 128
VC_C5 = 256
VC_C31 = 384

CU_COL = {"q": 0, "k": DD, "v": 2 * DD, "z": ST_END, "a": Z_END, "g": Z_END + DC}
CU_TILE = {"q": 0, "k": 8, "v": 16}
GATE_STEPS = ["bsig", "ny", "nex", "nln", "gg", "pref", "eall", "nbe"]

WINDOWS = [[("k", CTX, 0), ("v", CTX, 0)]] + [
    [("k", CTX, n), ("v", CTX, n), ("a", LAT, n - 1), ("g", LAT, n - 1)] for n in (1, 2, 3)] + [
    [("a", LAT, 3), ("g", LAT, 3), ("k", LAT, 0), ("v", LAT, 0), ("q", LAT, 0), ("z", LAT, 0)]] + [
    [("k", LAT, n), ("v", LAT, n), ("q", LAT, n), ("z", LAT, n)] for n in (1, 2, 3)]
CUS = [cu for w in WINDOWS for cu in w]
PAIRS = [(CTX, p) for p in range(NP)] + [(LAT, p) for p in range(NP)]
WO_FIRST = [(c, kg) for c in (0, 1) for kg in (4, 5, 6, 7, 0, 1, 2)]
WO_REST = [(0, 3), (1, 3)] + [(c, kg) for c in (2, 3) for kg in (4, 5, 6, 7, 0, 1, 2, 3)]


def delta_chunks(s, p):
    lat = s == LAT
    both = range(NT)
    ch = []
    for w in ("k", "q") if lat else ("k",):
        start = [("nsq", (s, w, p)), ("nrt", (s, w, p))]
        if ch:
            ch[-1] += start
        else:
            ch.append(start)
        ch.append([("nrc", (s, w, p)), ("kn", (s, w, p))])
    ch.append([])
    ch.append([("kT", (s, p)), ("kTc", (s, p))])
    if lat:
        ch.append([("qT", (p, 0)), ("qTc", (p, 0)), ("qdec", (p, 1)), ("qT", (p, 1)), ("qTc", (p, 1)),
                   ("qdec", (p, 2)), ("qT", (p, 2)), ("qTc", (p, 2))])
    decays = [(s, p, t, k) for t in both for k in range(1 + lat)]
    ch[-1].append(("gm", decays[0]))
    for n, key in enumerate(decays):
        ch.append([("dec", key)])
        k = key[:3]
        if key[3] == lat:
            ch[-1].append(("kk", k))
        if n + 1 < len(decays):
            ch[-1].append(("gm", decays[n + 1]))
        if key[3] == lat:
            ch[-1] += [("edec", k), ("gk", k), ("mneg", k), ("mhi", k)]
            ch[-1] += ([("attn", k[1:])] if lat else []) + [("mk", (*k, 0))]
    ch.append([("z", (s, p, t, 0)) for t in both] + [("yone", (s, p, t)) for t in both])
    ch.append([x for t in both for x in (("xadd", (s, p, t, 0)), ("mk", (s, p, t, 1)))])
    for l in range(1, LEVELS):
        ch.append([("z", (s, p, t, l)) for t in both])
        ch.append([(k, (s, p, t, l)) for k in ("zc", "xy") for t in both] + [x for t in both for x in (
            ("xadd", (s, p, t, l)), ("yadd", (s, p, t, l)),
            ("mk", (s, p, t, l + 1)) if l + 1 < LEVELS else ("mlo", (s, p, t)))])
    ch.append([("nr", (s, p, t)) for t in both] + [("nrr", (s, p, t)) for t in both])
    ch.append([])
    ch.append([("nx", (s, p, t)) for t in both])
    ch.append([("xf", (s, p, t)) for t in both])
    for i in range(NT):
        first, last = (not lat and i == 0), (lat and i == 1)
        ch.append([("vb", (s, p, i))] + ([] if last else [("kd", (s, p, i))]) + ([] if first else [("ks", (s, p, i))]))
        ch.append(([] if first else [("r", (s, p, i))]) + [("vn", (s, p, i))])
        ch.append([("vnc", (s, p, i))] + ([] if last else [("st", (s, p, i)), ("stc", (s, p, i))]))
    if lat:
        ch.append([("o", (p,)), ("oc", (p,)), ("osq", (p,)), ("ort", (p,))])
        ch.append([("orc", (p,)), ("on", (p,))])
        ch.append([("oT", (p,)), ("ym", (p,)), ("mix_hi", (p,)), ("mix_lo", (p,))])
    return ch


def norm_chunks():
    ch = [[("lnm", ())], [("cen", ())], [("csq", (0,))]]
    ch += [[("lnv", (i,)), ("lva", (i,))] + ([("csq", (i + 1,))] if i < 3 else []) for i in range(4)]
    ch += [[("lsd", ()), ("lnr", ()), ("lnn", ())]]
    ch += [[("lny", (i,)), ("mix_hi", (NP + i,)), ("mix_lo", (NP + i,))] for i in range(4)]
    return ch


def evacuation(cu):
    what, s, p = cu
    if what in "kvq":
        return [("tap2", cu), ("tapa", cu)], [(2, [("taps", cu)]), (4, [("csilu", cu)]), (6, [("nat", cu), ("natc", cu)])], []
    if what == "z":
        return [("zsilu", cu)], [], []
    if what == "a":
        return [], [], []
    return [("sg", (p,)), ("u", (p,))], [], [[("dw", (p, n))] for n in range(NDW)]


def turn_steps(s):
    return [(k, (s, kp)) for kp in range(8) for k in ("hf", "hhi", "hlo")]


def make_plan():
    plan = [("masks", ()), ("csil", ()), ("c4h", ()), ("c4l", ())]
    mr = [("mr", m, j) for m in range(16) for j in range(8)]

    def unit(u, halves=1, beside=lambda: None):
        plan.extend([("hi", (u,)), ("lo", (u,))])
        for half in range(halves):
            plan.append(("mm", (u, half)))
            beside()

    pieces = []
    soon = []
    late = []
    slot = [0, 0, 0]

    def beside():
        slot[0] += 1
        for n in range(2):
            level = pieces and pieces[0] and pieces[0][0][0] in ("z", "zc")
            if pieces and (n == 0 or (len(pieces) > slot[1] - slot[0] + SLACK and not level)):
                if n == 0 and level and (pieces[0][0][0] == "z") == (slot[0] % 2 == 0):
                    break
                plan.extend(pieces.pop(0))
                if level:
                    break
        if soon and slot[0] >= soon[0][0]:
            plan.extend(soon.pop(0)[1])
        if late and (slot[0] % 2 == 1 or 2 * len(late) > slot[2] - slot[0]):
            plan.extend(late.pop(0))

    def close():
        m = 16 if not mr else mr[0][1]
        if m and ("mcol", (m - 1,)) not in plan:
            plan.extend([("mcol", (m - 1,)), ("mcc", (m - 1,))])

    def gates(n):
        for _ in range(n):
            if mr:
                if mr[0][2] == 3:
                    close()
                plan.append(("macc", mr.pop(0)[1:]))

    turns = [(k, (s, kp)) for s in (CTX, LAT) for kp in range(8) for k in ("xT", "xTc")]
    for half in range(2):
        for j in range(KT):
            for q in range(2):
                unit(("mod", half, j, q))
                if (half, j, q) == (0, 4, 1):
                    plan.extend([("lvl", ()), ("cst", ()), ("vT", (0,)), ("vTc", (0,)), ("vT", (1,)), ("vTc", (1,)),
                                 ("nega", ())])
                if half == 0 and q == 1 and 7 <= j < 11:
                    s, t = divmod(j - 7, 2)
                    plan.append(("xsq", (s, t)))
                    if t == 1:
                        plan.extend([("xrt", (s,)), ("xrc", (s,)), ("xn", (s, 0)), ("xn", (s, 1))])
                if half == 1 and turns and (q or j % 4 == 3):
                    plan.extend([turns.pop(0), turns.pop(0)])
        plan.append(("mrow", (half,)))
    assert not turns
    plan.extend([("modcol", ()), ("s1", ())])
    plan.extend(turn_steps(CTX))
    for n, window in enumerate(WINDOWS):
        if n:
            pieces += delta_chunks(*PAIRS[n - 1])
        slot[1] = slot[0] + 8 * len(window)
        for k, cu in enumerate(window):
            rest = [c[0] for c in window[k:]]
            slot[2] = slot[0] + 8 * (rest.index("g") + 1 if "g" in rest else len(rest))
            for g in range(4):
                unit(("win", cu, g), 2, beside)
                gates(1 if n == 0 else g % 2 if n < 5 else 1 + g % 2)
                if (n, k) == (0, 0):
                    plan.extend(turn_steps(LAT)[6 * g:6 * g + 6])
            now, then, later = evacuation(cu)
            plan.extend(now)
            soon += [(slot[0] + wait, steps) for wait, steps in then]
            late += later
            if cu == ("g", LAT, 3):
                late += norm_chunks()
            if n == 0:
                unit(("ba", k))
                plan.extend([(x, (k,)) for x in GATE_STEPS])
        for _, steps in soon:
            plan.extend(steps)
        soon.clear()
    assert not late
    pieces += delta_chunks(LAT, 3)
    slot[1] = slot[0] + 2 * len(WO_FIRST)
    for c, kg in WO_FIRST:
        unit(("wo", c, kg), 2, beside)
        gates(1)
    for piece in pieces:
        plan.extend(piece)
    gates(len(mr))
    close()
    for q in range(4):
        plan.extend([("gdiag", (0, q)), ("gb", (0, q)), ("gbc", (0, q))])
    plan.append(("s2", ()))
    for c, kg in WO_REST:
        unit(("wo", c, kg), 2)
        if (c, kg) == (2, 5):
            plan.extend([(k, (t, i)) for i in (0, 1) for t in range(NT) for k in ("ysq", "yg")])
        if (c, kg) == (3, 5):
            plan.extend([(k, (t, 2)) for t in range(NT) for k in ("ysq", "yg")])
    plan.extend([("ysq", (t, 3)) for t in range(NT)] + [("ysm", ()), ("yrt", ())])
    plan.extend([("yg", (t, 3)) for t in range(NT)] + [("yrc", ())])
    plan.extend([(k, (t, c)) for t in range(NT) for c in range(4) for k in ("pn", "psq")])
    plan.extend([("psm", ()), ("xrt", (FFN,)), ("xrc", (FFN,)), ("xdg", ())])
    plan.extend([(k, (FFN, kp)) for kp in range(8) for k in ("xT", "fm", "fhi", "flo")])
    for q in range(4):
        plan.extend([("gdiag", (1, q)), ("gb", (1, q)), ("gbc", (1, q))])
    plan = splits_ahead(plan)
    ring = [key[0] if kind == "hi" else ("mr", *key) for kind, key in plan if kind in ("hi", "macc")]
    return plan, ring


def splits_ahead(plan):
    units = [key[0] for kind, key in plan if kind == "hi"]
    rest = [step for step in plan if step[0] not in ("hi", "lo")]
    firsts = [n for n, (kind, key) in enumerate(rest) if kind == "mm" and key[1] == 0]
    after = dict(zip(firsts, firsts[1:] + [len(rest)]))
    moved, placed, current = [], {"hi": 0, "lo": 0}, -1

    def split(kind, last):
        while placed[kind] < len(units) and placed[kind] <= last:
            moved.append((kind, (units[placed[kind]],)))
            placed[kind] += 1

    for n, (kind, key) in enumerate(rest):
        if n in after:
            current += 1
            levels = any(step[0] in ("zc", "yadd") for step in rest[n:after[n]])
            ahead = AHEAD - 1 if levels else AHEAD
            split("hi", current + ahead)
            split("lo", current + ahead)
        moved.append((kind, key))
        if kind == "yadd" and key[2] == NT - 1:
            split("hi", min(placed["hi"], current + AHEAD + 1))
        if kind == "zc" and key[2] == NT - 1:
            split("lo", min(placed["lo"], placed["hi"] - 1))
    return moved


def released_by(kind, key):
    if kind == "xy":
        return None
    return {
        "vT": ("vTc", key), "modcol": ("s1", ()), "xT": ("fm" if key and key[0] == FFN else "xTc", key), "pref": ("eall", key), "nat": ("natc", key),
        "kT": ("kTc", key), "qT": ("qTc", key), "dec": ("edec", key[:3]), "kk": ("gk", key),
        "z": ("xadd" if key and key[-1] == 0 else "zc", key), "nr": ("nrr", key), "nx": ("xf", key),
        "ks": ("r", key), "vn": ("vnc", key), "st": ("stc", key), "o": ("oc", key), "oT": ("ym", key),
        "lnm": ("cen", ()), "lnv": ("lva", key), "mcol": ("mcc", key), "gb": ("gbc", key),
    }.get(kind)


def count_steps():
    plan, ring = make_plan()
    count, totals = {}, {}
    for kind, key in plan:
        assert (kind, key) not in count, (kind, key)
        totals[kind] = totals.get(kind, 0) + 1
        count[kind, key] = totals[kind]
    bank, before, reader = {}, {}, {}
    free = [(b, None) for b in range(4, 8)]
    for kind, key in plan:
        if kind == "xy":
            uses = [((kind, key, "x"), ("xadd", key)), ((kind, key, "y"), ("yadd", key))]
        else:
            r = released_by(kind, key)
            uses = [((kind, key), r)] if r and not (kind == "dec" and key[3] == 1) else []
        for use, release in uses:
            assert free, use
            bank[use], before[use] = free.pop(0)
            reader[release] = bank[use]
        if (kind, key) in reader:
            free.append((reader.pop((kind, key)), (kind, key)))
    assert not reader
    return plan, ring, count, totals, bank, before


def layer(nc, x, cond, ctx, c_ctx, w_mod, b_mod, mix_norm_pre, mix_norm_post, w_in, qkv_conv, a_log, dt_bias,
          delta_out_norm, conf_dw, conf_ln_w, conf_ln_b, w_out, ffn_norm_pre, ffn_norm_post, w_gate, w_up,
          w_down, out):
    PLAN, RINGED, COUNT, TOTALS, BANK, BEFORE = count_steps()
    at_ring = {u: n for n, u in enumerate(RINGED)}
    UNITS = [u for u in RINGED if u[0] != "mr"]
    at_unit = {u: n for n, u in enumerate(UNITS)}

    es = ExitStack()
    with es:
        def alloc(stack):
            return lambda name, shape, dt=F32: stack.enter_context(nc.sbuf_tensor(name, [P, *shape], dt))

        sb = alloc(es)
        h_hi = sb("h_hi", [KT, T], F32R)
        h_lo = sb("h_lo", [KT, T], F32R)
        raw = sb("raw", [RING, UN])
        w_hi = sb("w_hi", [RING, UN], F32R)
        w_lo = sb("w_lo", [RING, UN], F32R)
        ident = sb("ident", [P])
        ones = sb("ones", [P])
        vcol = sb("vcol", [632])
        sh1 = sb("sh1", [KT, 2])
        sc1 = sb("sc1", [KT, 2])
        sc2 = sb("sc2", [KT])
        modc = sb("modc", [64])
        gw = sb("gw", [2, KT])
        csil = sb("csil", [2, KT])
        cst = sb("cst", [4])
        sums = sb("sums", [24])
        rstd = sb("rstd", [16])
        rtmp = sb("rtmp", [16])

        with ExitStack() as mixer:
            mb = alloc(mixer)
            hc_hi = mb("hc_hi", [KT, T], F32R)
            hc_lo = mb("hc_lo", [KT, T], F32R)
            mhi = mb("mhi", [NT, 4, P], F32R)
            mkl = mb("mkl", [NT, 4, P], F32R)
            xi = mb("xi", [NT, 4, P], F32R)
            yi = mb("yi", [NT, 4, P], F32R)
            zi = mb("zi", [NT, 4, P], F32R)
            id_r = mb("id_r", [P], F32R)
            nid_r = mb("nid_r", [P], F32R)
            c4 = mb("c4", [KT, 4], F32R)
            m_le, m_ge, m_lt, m_gt = (mb(f"m_{n}", [P]) for n in ("le", "ge", "lt", "gt"))
            lvl = mb("lvl", [LEVELS, P])
            gates_ = {s: {n: mb(f"{n}{s}", [2, NT, H]) for n in ("beta", "g", "nbeta", "y0", "y1", "y2")}
                      for s in (CTX, LAT)}
            ex = [mb(f"ex{s}", [3, 2, NT, H]) for s in (CTX, LAT)]
            nega = mb("nega", [16])
            dtb = mb("dtb", [16])
            macc = mb("macc", [2, 512])
            with ExitStack() as start:
                st = alloc(start)
                xs = [st("xs_ctx", [NT, D]), st("xs_lat", [NT, D])]
                modrow = st("modrow", [2 * D])
                hfs = st("hfs", [2, 2, T])
                vnat = st("vnat", [5, P])
                sel = st("sel", [2])
                ix = st("ix", [2, P], I32)
                lt = st("lt", [P])
            kvq = {w: mb(f"{w}n", [2, NT, 2, P]) for w in "kvq"}
            kTs = mb("kTs", [NT, 2, P])
            sil = mb("sil", [2, 2, T])
            zs = mb("zs", [2, 2, T])
            e_ = mb("e_", [4, P])
            mn = mb("mn", [NT, 4, P])
            sctx = mb("sctx", [NP, 4, P])
            vnew = mb("vnew", [NT, 4, P])
            rb = mb("rb", [4, P])
            kd = mb("kd", [4, P])
            gmv, tmp = kd[:, :, :].rearrange("p (d h) c -> p d h c", d=2), kd[:, :, :].rearrange("p a b -> p (a b)")
            with ExitStack() as conf:
                cf = alloc(conf)
                cacc = cf("cacc", [8, T])
                sgb = cf("sgb", [512])
                ub = cf("ub", [512])
                cx = cf("cx", [2, T])
            qx = mb("qx", [NT, 2, P])
            qTs = mb("qTs", [3, NT, 2, P])
            at = mb("at", [NT, 2, 2, P])
            slat = mb("slat", [4, P])
        act_hi = sb("act_hi", [FT, T], F32R)
        with ExitStack() as pre:
            dg = alloc(pre)("dg", [NT, P])
            hf2 = alloc(pre)("hf2", [2, 2, T])
            junk2 = alloc(pre)("junk2", [4, 512])
        act_lo = sb("act_lo", [FT, T], F32R)
        x1 = sb("x1", [NT, D])
        gw_all = sb("gw_all", [D])
        sgf = sb("sgf", [NT, 512])
        anf = sb("anf", [NT, 512])

        PS = es.enter_context(nc.psum_tensor("PS", [P, 8, 512], F32))

        def sem(name):
            return es.enter_context(nc.semaphore(name))

        S = {kind: sem(f"s_{kind}") for kind in TOTALS}
        landed = [sem(f"landed{i}") for i in range(RING)]
        small_in = {n: sem(f"in_{n}") for n in ("vec", "c", "dt", "bmod", "x0", "x1")}
        x_again, out_done = sem("x_again"), sem("out_done")
        ch_pool, ch_dve = sem("ch_pool"), sem("ch_dve")
        f_mm, f_sg, f_an, f_tr, f_ah, f_al, f_sq, f_yg, f_rt, f_rc, f_out = (
            sem(f"f_{n}") for n in ("mm", "sg", "an", "tr", "ah", "al", "sq", "yg", "rt", "rc", "out"))

        def need(eng, kind, *key):
            eng.wait_ge(S[kind], COUNT[kind, key])

        def bc(ap, axis, n):
            ap = ap.unsqueeze(axis)
            shape = list(ap.shape)
            shape[axis] = n
            return ap.to_broadcast(shape)

        def aux(eng, kind, key, part=None):
            use = (kind, key) if part is None else (kind, key, part)
            if BEFORE[use]:
                need(eng, BEFORE[use][0], *BEFORE[use][1])
            return BANK[use]

        def first_read(what):
            if what[0] == "ba":
                return [("bsig", what[1:]), ("ny", what[1:])]
            return {"a": [("u", what[2:])], "g": [("sg", what[2:])], "z": [("zsilu", what)]}.get(
                what[0], [("taps", what)])

        projected = []
        for u in RINGED:
            if u[0] == "ba" or (u[0] == "win" and u[2] == 0):
                projected.append(u if u[0] == "ba" else u[1])
        proj_bank = {w: n % 4 for n, w in enumerate(projected)}
        last_unit = {w: (w, 0) if w[0] == "ba" else (("win", w, 3), 1) for w in projected}
        conv_cus = [cu for cu in CUS if cu[0] in "kvq"]
        split_before = {}
        for n, u in enumerate(UNITS):
            split_before[u] = UNITS[n - RING] if n >= RING else None

        def last_mm(u):
            return (u, 1) if u[0] in ("win", "wo") else (u, 0)

        def projection(eng, what):
            need(eng, "mm", *last_unit[what])
            return PS[:, proj_bank[what], :]

        def unit_size(u):
            return KT * 4 * H if u[0] == "ba" else UN

        def wide(u, n):
            return w_hi[:, at_unit[u] % RING, 0:n], w_lo[:, at_unit[u] % RING, 0:n]

        w_mod_v = w_mod[0].rearrange("(p j) n -> p j n", j=KT)
        w_in_v = w_in[0].rearrange("(k p) n -> p k n", p=P)
        w_out_v = w_out[0].rearrange("(k p) n -> p k n", p=P)
        w_gate_v = w_gate[0].rearrange("(k p) n -> p k n", p=P)
        w_up_v = w_up[0].rearrange("(k p) n -> p k n", p=P)
        w_down_v = w_down[0].rearrange("(k p) n -> p k n", p=P)
        x_v = x[0].rearrange("(t p) n -> p t n", p=P)
        out_v = out[0].rearrange("(t p) n -> p t n", p=P)

        def unit_source(u):
            if u[0] == "mod":
                _, half, j, q = u
                return w_mod_v[:, j, half * D + q * UN:half * D + (q + 1) * UN]
            if u[0] == "ba":
                return w_in_v[:, :, 3 * DD:ST_END]
            if u[0] == "win":
                (what, _, p), g = u[1:]
                col = CU_COL[what] + 256 * p
                return w_in_v[:, 4 * g:4 * g + 4, col:col + 256]
            if u[0] == "wo":
                return w_out_v[:, 2 * u[2]:2 * u[2] + 2, 512 * u[1]:512 * (u[1] + 1)]
            return w_mod_v[:, 2 * u[2]:2 * u[2] + 2, 2 * D + 512 * u[1]:2 * D + 512 * (u[1] + 1)]

        def tile_of(d, i):
            return i if d == 0 else 1 - i

        R0, B0 = len(RINGED), TOTALS["hi"]
        NG = FC * 16
        ND = 4 * (FT // 2)

        seq_h = {CTX: (hc_hi, hc_lo), LAT: (h_hi, h_lo), FFN: (h_hi, h_lo)}

        block = es.enter_context(nc.Block())

        @block.sync
        def _(sp):
            sp.dma_start(csil[:, CTX, :], c_ctx.rearrange("(p j) -> p j", j=KT)).then_inc(small_in["c"], 16)
            sp.dma_start(csil[:, LAT, :], cond[0].rearrange("(p j) -> p j", j=KT)).then_inc(small_in["c"], 16)
            for n, u in enumerate(RINGED):
                if n >= RING:
                    old = RINGED[n - RING]
                    if old[0] == "mr":
                        need(sp, "macc", *old[1:])
                    else:
                        need(sp, "hi", old)
                        need(sp, "lo", old)
                src = unit_source(u)
                dst = raw[:, n % RING, 0:unit_size(u)]
                if len(src.shape) == 3:
                    dst = dst.rearrange("p (a b) -> p a b", a=src.shape[1])
                sp.dma_start(dst, src).then_inc(landed[n % RING], 16)
                if n == 8:
                    for s, a in ((0, ctx), (1, x)):
                        sp.dma_start(xs[s][:, :, :], a[0].rearrange("(t p) n -> p t n", p=P)).then_inc(
                            small_in[f"x{s}"], 16)

            def gate_up(c, c16):
                for i in range(16):
                    sp.wait_ge(S["hi"], B0 - RING + 1 + i + c16)
                    sp.wait_ge(S["lo"], B0 - RING + 1 + i + c16)
                    src = w_gate_v if i < 8 else w_up_v
                    k = 2 * (i % 8)
                    cols = slice(c * 512, (c + 1) * 512) if isinstance(c, int) else ds(c * 512, 512)
                    sp.dma_start(raw[:, (R0 + i) % RING, :].rearrange("p (a b) -> p a b", a=2),
                                 src[:, k:k + 2, cols]).then_inc(landed[(R0 + i) % RING], 16)

            gate_up(0, 0)
            with sp.Fori(1, FC) as c:
                gate_up(c, c * 16)
            for v in range(ND):
                U = NG + v
                sp.wait_ge(S["hi"], B0 + U - RING + 1)
                sp.wait_ge(S["lo"], B0 + U - RING + 1)
                cc, g = divmod(v, FT // 2)
                sp.dma_start(raw[:, (R0 + U) % RING, :].rearrange("p (a b) -> p a b", a=2),
                             w_down_v[:, 2 * g:2 * g + 2, 512 * cc:512 * (cc + 1)]).then_inc(
                    landed[(R0 + U) % RING], 16)
            for n in range(8):
                t, cc = divmod(n, 4)
                sp.wait_ge(f_out, n + 1)
                sp.dma_start(out_v[:, t, 512 * cc:512 * (cc + 1)], x1[:, t, 512 * cc:512 * (cc + 1)]).then_inc(
                    out_done, 16)
            sp.wait_ge(out_done, 16 * 8)

        @block.gpsimd
        def _(pool):
            n_chain = [0]

            def link(ins):
                n_chain[0] += 1
                ins.then_inc(ch_pool, 1)
                pool.wait_ge(ch_pool, n_chain[0])

            def masks():
                pool.memset(sel[:, :], 0.0)
                pool.memset(ident[:, :], 0.0)
                link(pool.memset(ones[:, :], 1.0))
                pool.iota(ix[:, 0, :], [[0, P]], base=0, channel_multiplier=1)
                pool.iota(ix[:, 1, :], [[1, P]], base=0, channel_multiplier=0)
                for m, sign, op in ((m_le, 1, ALU.is_ge), (m_lt, 1, ALU.is_gt), (m_ge, -1, ALU.is_ge),
                                    (m_gt, -1, ALU.is_gt)):
                    pool.affine_select(out=m[:, :], in_=ones[:, :], compare_op=op, fill=0.0, base=0,
                                       pattern=[[sign, P]], channel_multiplier=-sign)
                pool.affine_select(out=ident[:, :], in_=ident[:, :], compare_op=ALU.not_equal, fill=1.0, base=0,
                                   pattern=[[-1, P]], channel_multiplier=1)
                for base, step in ((0, -1), (-2, -1)):
                    link(pool.affine_select(out=sel[:, :], in_=sel[:, :], compare_op=ALU.not_equal, fill=1.0,
                                            base=base, pattern=[[step, 2]], channel_multiplier=1))
                pool.affine_select(out=sel[:, :], in_=sel[:, :], compare_op=ALU.not_equal, fill=1.0, base=-4,
                                   pattern=[[0, 2]], channel_multiplier=1).then_inc(S["masks"], 1)

            def small_loads():
                for r, (v, n) in enumerate(((mix_norm_pre, 16), (ffn_norm_pre, 16), (mix_norm_post, 16),
                                            (ffn_norm_post, 16), (conf_ln_w, 8), (conf_ln_b, 8),
                                            (delta_out_norm, 1))):
                    row = (0, 16, 32, 48, 64, 72, 80)[r]
                    pool.dma_start(vnat[row:row + n, 0, :], v[0].rearrange("(a b) -> a b", b=P)).then_inc(
                        small_in["vec"], 16)
                pool.dma_start(vnat[0:64, 1, :], b_mod[0, 2 * D:6 * D].rearrange("(a b) -> a b", b=P)).then_inc(
                    small_in["vec"], 16)
                pool.dma_start(vnat[0:120, 2, :], qkv_conv[0].rearrange("w (a b) -> (w a) b", b=P)).then_inc(
                    small_in["vec"], 16)
                dw = conf_dw[0].rearrange("w (a b) -> (w a) b", b=P)
                pool.dma_start(vnat[0:124, 3, :], dw[0:124, :]).then_inc(small_in["vec"], 16)
                pool.dma_start(vnat[0:124, 4, :], dw[124:248, :]).then_inc(small_in["vec"], 16)
                pool.dma_start(nega[:, :], a_log[0].rearrange("a b -> (a b)").partition_broadcast(P)).then_inc(
                    small_in["dt"], 16)
                pool.dma_start(dtb[:, :], dt_bias[0].rearrange("a b -> (a b)").partition_broadcast(P)).then_inc(
                    small_in["dt"], 16)
                pool.dma_start(modrow[4:5, :], b_mod[0:1, 0:2 * D]).then_inc(small_in["bmod"], 16)

            small_loads()
            for kind, key in PLAN:
                if kind == "masks":
                    masks()
                elif kind == "xn":
                    s, t = key
                    need(pool, "xrc", s)
                    pool.tensor_scalar(xs[s][:, t, :], xs[s][:, t, :], rstd[:, 2 * s + t:2 * s + t + 1], None,
                                       ALU.mult).then_inc(S[kind], 1)
                elif kind == "gm":
                    s, p, t, k = key
                    need(pool, "gg", s)
                    if (t, k) != (0, 0):
                        pool.wait_ge(S["dec"], COUNT["gm", key] - 1)
                    else:
                        need(pool, "nsq", s, "q" if s == LAT else "k", p)
                    for d, m in enumerate(((m_gt, m_lt), (m_le, m_ge))[k]):
                        ins = pool.tensor_tensor(gmv[:, d, :, :], bc(m[:, :], 1, 2),
                                                 bc(gates_[s]["g"][:, d, t, 2 * p:2 * p + 2], 2, P), ALU.mult)
                    ins.then_inc(S[kind], 1)
                elif kind == "qdec":
                    p, k = key
                    need(pool, "kn", LAT, "q", p)
                    need(pool, "eall", LAT)
                    if k == 2:
                        need(pool, "qT", p, 1)
                    elif p:
                        need(pool, "qT", p - 1, 2)
                    else:
                        need(pool, "mix_lo", NP + 3)
                    par = PAIRS.index((LAT, p)) % 2
                    pool.tensor_tensor(qx[:, :, :, :], kvq["q"][:, par, :, :, :],
                                       bc(ex[LAT][:, 0, k - 1, :, 2 * p:2 * p + 2], 3, P), ALU.mult).then_inc(S[kind], 1)
                elif kind == "attn":
                    p, t = key
                    need(pool, "gk", LAT, p, t)
                    if p:
                        need(pool, "o", p - 1)
                    else:
                        need(pool, "mix_lo", NP + 3)
                    for d, m in enumerate((m_le, m_ge)):
                        ins = pool.tensor_tensor(at[:, t, d, :, :], e_[:, 2:4, :], bc(m[:, :], 1, 2), ALU.mult)
                    ins.then_inc(S[kind], 1)
                elif kind == "mk":
                    s, p, t, l = key
                    need(pool, "mhi", s, p, t)
                    need(pool, "lvl")
                    if l:
                        need(pool, "z", s, p, t, l - 1)
                        if l == 1:
                            need(pool, "yone", s, p, t)
                    elif (s, p) != PAIRS[0]:
                        need(pool, "nr", *PAIRS[PAIRS.index((s, p)) - 1], t)
                    pool.tensor_tensor(mkl[:, t, :, :], mhi[:, t, :, :].bitcast(F32), bc(lvl[:, l, :], 1, 4),
                                       ALU.mult).then_inc(S[kind], 1)
                elif kind == "mlo":
                    s, p, t = key
                    need(pool, "z", s, p, t, LEVELS - 1)
                    need(pool, "mneg", s, p, t)
                    pool.tensor_tensor(mkl[:, t, :, :], mn[:, t, :, :], mhi[:, t, :, :].bitcast(F32),
                                       ALU.subtract).then_inc(S[kind], 1)
                elif kind == "vb":
                    s, p, i = key
                    par = PAIRS.index((s, p)) % 2
                    need(pool, "natc", "v", s, p)
                    need(pool, "bsig", s)
                    if (s, p, i) != (CTX, 0, 0):
                        prev = (s, p, i - 1) if i else (*PAIRS[PAIRS.index((s, p)) - 1], 1)
                        need(pool, "vn", *prev)
                        if i == 0 and prev[0] == LAT:
                            need(pool, "oT", prev[1])
                    for d in range(2):
                        ins = pool.tensor_tensor(rb[:, 2 * d:2 * d + 2, :], kvq["v"][:, par, tile_of(d, i), :, :],
                                                 bc(gates_[s]["beta"][:, d, tile_of(d, i), 2 * p:2 * p + 2], 2, P),
                                                 ALU.mult)
                    ins.then_inc(S[kind], 1)
                elif kind == "kd":
                    s, p, i = key
                    par = PAIRS.index((s, p)) % 2
                    need(pool, "kn", s, "k", p)
                    need(pool, "eall", s)
                    if i:
                        need(pool, "st", s, p, 0)
                    else:
                        need(pool, "dec", s, p, 1, 1 if s == LAT else 0)
                    for d in range(2):
                        ins = pool.tensor_tensor(kd[:, 2 * d:2 * d + 2, :], kvq["k"][:, par, tile_of(d, i), :, :],
                                                 bc(ex[s][:, 1, d, tile_of(d, i), 2 * p:2 * p + 2], 2, P), ALU.mult)
                    ins.then_inc(S[kind], 1)
                elif kind == "s2":
                    need(pool, "mix_lo", NP - 1)
                    pool.dma_start(x1[:, :, :], x_v).then_inc(x_again, 16)

        @block.scalar
        def _(act):
            def copy(out_ap, in_ap, kind):
                act.activation(out_ap, in_ap, ACT.Copy).then_inc(S[kind], 1)

            def gate_spread(w, q):
                need(act, "gb", w, q)
                if (w, q) == (1, 0):
                    need(act, "pn", 1, 3)
                copy(gw_all[:, 512 * q:512 * (q + 1)], PS[:, BANK["gb", (w, q)], :], "gbc")

            for kind, key in PLAN:
                if kind == "vTc":
                    n, = key
                    need(act, "vT", n)
                    b = BANK["vT", key]
                    if n == 0:
                        act.activation(vcol[:, 0:81], PS[:, b, 0:81], ACT.Copy)
                        act.activation(vcol[:, VC_MOD:VC_MOD + 64], PS[:, b, 128:192], ACT.Copy)
                        copy(vcol[:, VC_C5:VC_C5 + 120], PS[:, b, 256:376], kind)
                    else:
                        copy(vcol[:, VC_C31:VC_C31 + 248], PS[:, b, 0:248], kind)
                elif kind == "csil":
                    act.wait_ge(small_in["c"], 32)
                    act.activation(csil[:, :, :], csil[:, :, :], ACT.Silu).then_inc(S[kind], 1)
                elif kind == "c4h":
                    need(act, "csil")
                    copy(c4[:, :, 0:2].rearrange("p j w -> p w j"), csil[:, :, :], kind)
                elif kind == "nega":
                    act.wait_ge(small_in["dt"], 32)
                    act.activation(nega[:, :], nega[:, :], ACT.Exp).then_inc(S[kind], 1)
                elif kind == "hi":
                    u, = key
                    n = at_ring[u]
                    act.wait_ge(landed[n % RING], 16 * (n // RING + 1))
                    if split_before[u]:
                        need(act, "mm", *last_mm(split_before[u]))
                    sz = unit_size(u)
                    copy(wide(u, sz)[0], raw[:, n % RING, 0:sz], kind)
                elif kind == "xsq":
                    s, t = key
                    act.wait_ge(small_in[f"x{s}"], 16)
                    if (s, t) == (0, 0):
                        need(act, "vTc", 1)
                    else:
                        act.wait_ge(S[kind], 2 * s + t)
                    act.activation(PS[:, 4:8, :].rearrange("p a b -> p (a b)"), xs[s][:, t, :], ACT.Square,
                                   accum_out=sums[:, 2 * s + t:2 * s + t + 1]).then_inc(S[kind], 1)
                elif kind == "xTc":
                    s, kp = key
                    need(act, "xT", *key)
                    copy(xs[s][:, :, T * kp:T * (kp + 1)],
                         PS[:, BANK["xT", key], :].rearrange("p (k t) -> p k t", k=2), kind)
                elif kind == "xrt":
                    s, = key
                    need(act, *(("psm",) if s == FFN else ("xsq", s, 1)))
                    need(act, "cst")
                    act.activation(rtmp[:, 2 * s:2 * s + 2], sums[:, 2 * s:2 * s + 2], ACT.Sqrt, bias=cst[:, 0:1],
                                   scale=1.0 / D).then_inc(S[kind], 1)
                elif kind == "mrow":
                    half, = key
                    need(act, "mm", ("mod", half, KT - 1, 1), 0)
                    copy(modrow[0:4, half * D:(half + 1) * D], PS[0:4, 0:4, :].rearrange("p a b -> p (a b)"), kind)
                elif kind == "hhi":
                    s, kp = key
                    hi, lo = seq_h[s]
                    need(act, "xTc", s, kp)
                    need(act, "s1")
                    for kt in (2 * kp, 2 * kp + 1):
                        ins = act.activation(hi[:, kt, :], xs[s][:, kt % 2, T * kp:T * (kp + 1)], ACT.Identity,
                                             scale=sc1[:, kt, s:s + 1], bias=sh1[:, kt, s:s + 1])
                    ins.then_inc(S[kind], 1)
                elif kind == "bsig":
                    s, = key
                    pr = projection(act, ("ba", s))[:, 0:64].rearrange("p (t n) -> p t n", t=NT)
                    for d in range(2):
                        ins = act.activation(gates_[s]["beta"][:, d, :, :], pr[:, :, 8 * d:8 * d + 8], ACT.Sigmoid)
                    ins.then_inc(S[kind], 1)
                elif kind == "nex":
                    s, = key
                    need(act, "ny", s)
                    y2 = gates_[s]["y2"][:, :, :, :]
                    act.activation(y2, y2, ACT.Exp).then_inc(S[kind], 1)
                elif kind == "nln":
                    s, = key
                    need(act, "nex", s)
                    y2 = gates_[s]["y2"][:, :, :, :]
                    act.activation(y2, y2, ACT.Ln, bias=cst[:, 2:3]).then_inc(S[kind], 1)
                elif kind == "eall":
                    s, = key
                    need(act, "pref", s)
                    act.activation(ex[s][:, :, :, :, :].rearrange("p a b c d -> p (a b c d)"),
                                   PS[:, BANK["pref", key], 0:96], ACT.Exp).then_inc(S[kind], 1)
                elif kind == "tap2":
                    n = conv_cus.index(key)
                    what, s, p = key
                    pr = projection(act, key)
                    if n >= 2:
                        need(act, "nat", *conv_cus[n - 2])
                    else:
                        need(act, "hlo", LAT, 7)
                    for h in range(2):
                        col = VC_C5 + 2 * 24 + CU_TILE[what] + 2 * p + h
                        ins = act.activation(sil[:, n % 2, h, :], pr[:, T * h:T * (h + 1)], ACT.Copy,
                                             scale=vcol[:, col:col + 1])
                    ins.then_inc(S[kind], 1)
                elif kind == "csilu":
                    n = conv_cus.index(key)
                    need(act, "tapa", *key)
                    need(act, "taps", *key)
                    act.activation(sil[:, n % 2, :, :], sil[:, n % 2, :, :], ACT.Silu).then_inc(S[kind], 1)
                elif kind == "natc":
                    what, s, p = key
                    need(act, "nat", *key)
                    k = PAIRS.index((s, p))
                    if k >= 2:
                        need(act, "vb", *PAIRS[k - 2], 1)
                    copy(kvq[what][:, k % 2, :, :, :].rearrange("p t h d -> p (t h d)"),
                         PS[:, BANK["nat", key], :], kind)
                elif kind == "zsilu":
                    p = key[2]
                    pr = projection(act, key)
                    if p >= 2:
                        need(act, "ym", p - 2)
                    act.activation(zs[:, p % 2, :, :].rearrange("p h t -> p (h t)"), pr, ACT.Silu).then_inc(S[kind], 1)
                elif kind == "nrt":
                    s, what, p = key
                    need(act, "nsq", *key)
                    a = 8 if what == "k" else 12
                    act.activation(rtmp[:, a:a + 4], sums[:, a:a + 4], ACT.Sqrt,
                                   bias=cst[:, 0:1] if what == "k" else cst[:, 1:2],
                                   scale=1.0 if what == "k" else float(P)).then_inc(S[kind], 1)
                elif kind == "kTc":
                    need(act, "kT", *key)
                    k = PAIRS.index(key)
                    if k:
                        need(act, "ks", *PAIRS[k - 1], 1)
                    copy(kTs[:, :, :, :].rearrange("p t h d -> p (t h d)"), PS[:, BANK["kT", key], :], kind)
                elif kind == "qTc":
                    p, k = key
                    need(act, "qT", p, k)
                    if p:
                        need(act, "o", p - 1)
                    copy(qTs[:, k, :, :, :].rearrange("p t h d -> p (t h d)"), PS[:, BANK["qT", key], :], kind)
                elif kind == "edec":
                    s, p, t = key
                    n = 4 if s == LAT else 2
                    need(act, "dec", s, p, t, n // 2 - 1)
                    if COUNT[kind, key] > 1:
                        act.wait_ge(S["mneg"], COUNT[kind, key] - 1)
                        if s == LAT and (p, t) != (0, 0):
                            need(act, "attn", *((p, 0) if t else (p - 1, 1)))
                    act.activation(e_[:, 0:n, :].rearrange("p a b -> p (a b)"),
                                   PS[:, BANK["dec", (s, p, t, 0)], 0:n * P], ACT.Exp).then_inc(S[kind], 1)
                elif kind == "mhi":
                    s, p, t = key
                    need(act, "mneg", s, p, t)
                    if (s, p) != PAIRS[0]:
                        need(act, "nr", *PAIRS[PAIRS.index((s, p)) - 1], t)
                    copy(mhi[:, t, :, :], mn[:, t, :, :], kind)
                elif kind == "zc":
                    t = key[2]
                    need(act, "z", *key)
                    k = PAIRS.index(key[:2])
                    if key[3] == 1 and k:
                        need(act, "nx", *PAIRS[k - 1], t)
                    copy(zi[:, t, :, :].rearrange("p a b -> p (a b)"), PS[:, BANK["z", key], :], kind)
                elif kind == "yadd":
                    t = key[2]
                    need(act, "xy", *key)
                    copy(yi[:, t, :, :].rearrange("p a b -> p (a b)"), PS[:, BANK["xy", key, "y"], :], kind)
                elif kind == "vnc":
                    s, p, i = key
                    need(act, "vn", *key)
                    if s == LAT and p:
                        need(act, "o", p - 1)
                    copy(vnew[:, i, :, :].rearrange("p a b -> p (a b)"), PS[:, BANK["vn", key], :], kind)
                elif kind == "oc":
                    need(act, "o", *key)
                    copy(rb[:, :, :].rearrange("p a b -> p (a b)"), PS[:, BANK["o", key], :], kind)
                elif kind == "ort":
                    need(act, "osq", *key)
                    act.activation(rtmp[:, 8:12], sums[:, 8:12], ACT.Sqrt, bias=cst[:, 0:1],
                                   scale=1.0 / P).then_inc(S[kind], 1)
                elif kind == "mix_hi":
                    n, = key
                    if n < NP:
                        need(act, "ym", n)
                        src = kd[:, :, :].rearrange("p a b -> p (a b)")
                    else:
                        need(act, "lny", n - NP)
                        src = ub[:, :]
                    if n == NP:
                        need(act, "mm", ("win", ("v", CTX, 3), 3), 1)
                    copy(hc_hi[:, 2 * n:2 * n + 2, :].rearrange("p a b -> p (a b)"), src, kind)
                elif kind == "sg":
                    i, = key
                    pr = projection(act, ("g", LAT, i))
                    if i:
                        need(act, "u", i - 1)
                    act.activation(sgb[:, :], pr, ACT.Sigmoid).then_inc(S[kind], 1)
                elif kind == "csq":
                    i, = key
                    if i:
                        need(act, "lnv", i - 1)
                    need(act, "cen")
                    act.activation(ub[:, :], cacc[:, 2 * i:2 * i + 2, :].rearrange("p a b -> p (a b)"),
                                   ACT.Square).then_inc(S[kind], 1)
                elif kind == "lsd":
                    need(act, "lva", 3)
                    act.activation(cx[:, 1, :], cx[:, 0, :], ACT.Sqrt, bias=cst[:, 0:1],
                                   scale=1.0 / DC).then_inc(S[kind], 1)
                elif kind == "lny":
                    i, = key
                    need(act, "lnn")
                    if i:
                        need(act, "mix_hi", NP + i - 1)
                        need(act, "mix_lo", NP + i - 1)
                    for h in range(2):
                        n = 2 * i + h
                        ins = act.activation(ub[:, T * h:T * (h + 1)], cacc[:, n, :], ACT.Silu,
                                             scale=vcol[:, VC_LNW + n:VC_LNW + n + 1],
                                             bias=vcol[:, VC_LNB + n:VC_LNB + n + 1])
                    ins.then_inc(S[kind], 1)
                elif kind == "gbc" and key[0] == 0:
                    gate_spread(*key)
                elif kind == "ysq":
                    t, c = key
                    need(act, "mm", ("wo", c, 3), 1)
                    n = COUNT[kind, key] - 1
                    if n >= 4:
                        act.wait_ge(S[kind], n - 3)
                    act.activation(junk2[:, n % 4, :], PS[:, 2 * c + t, :], ACT.Square,
                                   accum_out=sums[:, 8 + 4 * t + c:9 + 4 * t + c]).then_inc(S[kind], 1)
                elif kind == "yrt":
                    need(act, "ysm")
                    act.activation(rtmp[:, 6:8], sums[:, 6:8], ACT.Sqrt, bias=cst[:, 0:1],
                                   scale=1.0 / D).then_inc(S[kind], 1)
                elif kind == "psq":
                    t, c = key
                    need(act, "pn", t, c)
                    n = COUNT[kind, key] - 1
                    if n >= 4:
                        act.wait_ge(S[kind], n - 3)
                    else:
                        need(act, "ysq", 1, 3)
                    act.activation(junk2[:, n % 4, :], x1[:, t, 512 * c:512 * (c + 1)], ACT.Square,
                                   accum_out=sums[:, 16 + 4 * t + c:17 + 4 * t + c]).then_inc(S[kind], 1)
                elif kind == "fm":
                    _, kp = key
                    need(act, "xT", FFN, kp)
                    need(act, "s2")
                    if kp >= 2:
                        need(act, "flo", FFN, kp - 2)
                    for k in range(2):
                        kt = 2 * kp + k
                        ins = act.activation(hf2[:, kp % 2, k, :], PS[:, BANK["xT", key], T * k:T * (k + 1)],
                                             ACT.Identity, scale=sc2[:, kt:kt + 1],
                                             bias=modc[:, KT + kt:KT + kt + 1])
                    ins.then_inc(S[kind], 1)

            def split(n, land, mm_done):
                act.wait_ge(landed[(R0 + n) % RING], land)
                act.wait_ge(f_mm, mm_done)
                copy(w_hi[:, (B0 + n) % RING, :], raw[:, (R0 + n) % RING, :], "hi")

            def turned_hi(cs, c1):
                act.wait_ge(f_tr, c1)
                for t in range(NT):
                    act.activation(act_hi[:, cs, P * t:P * (t + 1)],
                                   PS[:, 4 + t, :].rearrange("p (a b) -> p a b", a=4), ACT.Copy).then_inc(f_ah, 1)

            def gate_up(c, static):
                for i in range(16):
                    n = R0 + i
                    slot = n % RING
                    if static and c == 0 and i < RING:
                        act.wait_ge(landed[slot], 16 * (n // RING + 1))
                        need(act, "mm", *last_mm(UNITS[B0 - RING + i]))
                        copy(w_hi[:, (B0 + i) % RING, :], raw[:, slot, :], "hi")
                    else:
                        split(i, c * 64 + 16 * (n // RING + 1), c * 16 + (i - RING + 1))
                    if static and c == 0 and 4 <= i < 8:
                        gate_spread(1, i - 4)
                    if i == 9 and not (static and c == 0):
                        turned_hi(slice(4 * (c - 1), 4 * c) if static else ds(c * 4 - 4, 4), c)
                    if i == 11:
                        act.wait_ge(f_mm, c * 16 + 8)
                        if not (static and c == 0):
                            act.wait_ge(f_an, c)
                        act.activation(sgf[:, :, :], PS[:, 0:2, :], ACT.Silu).then_inc(f_sg, 1)

            gate_up(0, True)
            gate_up(1, True)
            with act.Fori(2, FC) as c:
                gate_up(c, False)
            for v in range(ND):
                n = R0 + NG + v
                split(NG + v, 16 * (n // RING + 1), NG + v - RING + 1)
                if v == 4:
                    turned_hi(slice(4 * (FC - 1), 4 * FC), FC)
                if v in (30, 52, 74):
                    cc = v // 22 - 1
                    act.wait_ge(f_mm, NG + 22 * (cc + 1))
                    for t in range(NT):
                        act.activation(sgf[:, t, :], PS[:, 2 * cc + t, :], ACT.Square,
                                       accum_out=sums[:, 8 + 4 * t + cc:9 + 4 * t + cc]).then_inc(f_sq, 1)
            act.wait_ge(f_mm, NG + ND)
            for t in range(NT):
                act.activation(sgf[:, t, :], PS[:, 6 + t, :], ACT.Square,
                               accum_out=sums[:, 11 + 4 * t:12 + 4 * t]).then_inc(f_sq, 1)
            act.wait_ge(f_rc, 1)
            act.activation(rtmp[:, 0:2], rtmp[:, 2:4], ACT.Sqrt, bias=cst[:, 0:1], scale=1.0 / D).then_inc(f_rt, 1)

        @block.vector
        def _(dve):
            n_chain = [0]

            def step(ins, lag=0):
                n_chain[0] += 1
                ins.then_inc(ch_dve, 1)
                if n_chain[0] > lag:
                    dve.wait_ge(ch_dve, n_chain[0] - lag)

            def four(ap):
                return ap.rearrange("p (a b) -> p a b", a=4)

            def gate_diagonal(w, q):
                need(dve, "mcc", 15)
                need(dve, "mix_lo", NP - 1)
                if (w, q) != (0, 0):
                    need(dve, "gb", *((w, q - 1) if q else (0, 3)))
                for i in range(4):
                    g = (0, 3 * KT)[w] + 4 * q + i
                    v = (VC_POST1, VC_POST2)[w] + 4 * q + i
                    ins = dve.tensor_scalar(sgf[:, 0, P * i:P * (i + 1)], ident[:, :], modc[:, g:g + 1],
                                            vcol[:, v:v + 1], ALU.mult, ALU.mult)
                ins.then_inc(S["gdiag"], 1)

            for kind, key in PLAN:
                done = S[kind]
                if kind == "lvl":
                    need(dve, "masks")
                    xr = ix[:, 0, :]
                    step(dve.tensor_tensor(xr, ix[:, 0, :], ix[:, 1, :], ALU.bitwise_xor))
                    step(dve.tensor_copy(lt[:, :], xr))
                    for l in range(LEVELS):
                        step(dve.tensor_scalar(lvl[:, l, :], lt[:, :], float(2 ** l), None, ALU.is_ge))
                        ins = dve.scalar_tensor_tensor(out=lvl[:, l, :], in0=lt[:, :], scalar=float(2 ** (l + 1)),
                                                       in1=lvl[:, l, :], op0=ALU.is_lt, op1=ALU.mult)
                    ins.then_inc(done, 1)
                elif kind == "cst":
                    dve.memset(cst[:, 0:1], EPS)
                    dve.memset(cst[:, 1:2], EPS * P)
                    dve.memset(cst[:, 2:3], 1.0)
                    dve.tensor_copy(id_r[:, :], ident[:, :])
                    dve.tensor_scalar(nid_r[:, :], ident[:, :], -1.0, None, ALU.mult).then_inc(done, 1)
                elif kind == "c4l":
                    need(dve, "c4h")
                    dve.tensor_tensor(c4[:, :, 2:4].rearrange("p j w -> p w j"), csil[:, :, :],
                                      c4[:, :, 0:2].bitcast(F32).rearrange("p j w -> p w j"),
                                      ALU.subtract).then_inc(done, 1)
                elif kind == "lo":
                    u, = key
                    need(dve, "hi", u)
                    sz = unit_size(u)
                    hi, lo = wide(u, sz)
                    dve.tensor_tensor(lo, raw[:, at_ring[u] % RING, 0:sz], hi.bitcast(F32),
                                      ALU.subtract).then_inc(done, 1)
                elif kind == "xrc":
                    s, = key
                    need(dve, "xrt", s)
                    dve.reciprocal(rstd[:, 2 * s:2 * s + 2], rtmp[:, 2 * s:2 * s + 2]).then_inc(done, 1)
                elif kind == "xdg":
                    need(dve, "xrc", FFN)
                    for t in range(NT):
                        ins = dve.tensor_scalar(dg[:, t, :], ident[:, :], rstd[:, 4 + t:5 + t], None, ALU.mult)
                    ins.then_inc(done, 1)
                elif kind == "fhi":
                    _, kp = key
                    need(dve, "fm", FFN, kp)
                    dve.tensor_copy(h_hi[:, 2 * kp:2 * kp + 2, :], hf2[:, kp % 2, :, :]).then_inc(done, 1)
                elif kind == "flo":
                    _, kp = key
                    need(dve, "fhi", FFN, kp)
                    dve.tensor_tensor(h_lo[:, 2 * kp:2 * kp + 2, :], hf2[:, kp % 2, :, :],
                                      h_hi[:, 2 * kp:2 * kp + 2, :].bitcast(F32), ALU.subtract).then_inc(done, 1)
                elif kind == "s1":
                    need(dve, "modcol")
                    ps = PS[:, BANK["modcol", ()], 0:64].rearrange("p (a b) -> p a b", b=2)
                    dve.tensor_copy(sh1[:, :, :], ps[:, 0:KT, :])
                    dve.scalar_tensor_tensor(out=sc1[:, :, :], in0=ps[:, KT:2 * KT, :], scalar=1.0,
                                             in1=bc(vcol[:, VC_PRE1:VC_PRE1 + KT], 2, 2), op0=ALU.add,
                                             op1=ALU.mult).then_inc(done, 1)
                elif kind == "s2":
                    need(dve, "mcc", 15)
                    dve.scalar_tensor_tensor(out=sc2[:, :], in0=modc[:, 2 * KT:3 * KT], scalar=1.0,
                                             in1=vcol[:, VC_PRE2:VC_PRE2 + KT], op0=ALU.add,
                                             op1=ALU.mult).then_inc(done, 1)
                elif kind == "hf":
                    s, kp = key
                    need(dve, "xTc", s, kp)
                    need(dve, "s1")
                    if kp >= 2:
                        need(dve, "hlo", s, kp - 2)
                    elif s == LAT:
                        need(dve, "hlo", CTX, kp + 6)
                    for k in range(2):
                        kt = 2 * kp + k
                        ins = dve.tensor_scalar(hfs[:, kp % 2, k, :], xs[s][:, k, T * kp:T * (kp + 1)],
                                                sc1[:, kt, s:s + 1], sh1[:, kt, s:s + 1], ALU.mult, ALU.add)
                    ins.then_inc(done, 1)
                elif kind == "hlo":
                    s, kp = key
                    need(dve, "hhi", s, kp)
                    need(dve, "hf", s, kp)
                    hi, lo = seq_h[s]
                    dve.tensor_tensor(lo[:, 2 * kp:2 * kp + 2, :], hfs[:, kp % 2, :, :],
                                      hi[:, 2 * kp:2 * kp + 2, :].bitcast(F32), ALU.subtract).then_inc(done, 1)
                elif kind == "ny":
                    s, = key
                    pr = projection(dve, ("ba", s))[:, 0:64].rearrange("p (t n) -> p t n", t=NT)
                    g = gates_[s]
                    need(dve, "bsig", s)
                    dve.wait_ge(small_in["dt"], 32)
                    for d in range(2):
                        ins = dve.tensor_tensor(g["y0"][:, d, :, :], pr[:, :, 16 + 8 * d:24 + 8 * d],
                                                bc(dtb[:, 8 * d:8 * d + 8], 1, NT), ALU.add)
                    step(ins)
                    step(dve.tensor_scalar(g["y1"][:, :, :, :], g["y0"][:, :, :, :], 0.0, None, ALU.max))
                    dve.scalar_tensor_tensor(out=g["y2"][:, :, :, :], in0=g["y1"][:, :, :, :], scalar=-2.0,
                                             in1=g["y0"][:, :, :, :], op0=ALU.mult, op1=ALU.add).then_inc(done, 1)
                elif kind == "gg":
                    s, = key
                    g = gates_[s]
                    need(dve, "nln", s)
                    need(dve, "ny", s)
                    need(dve, "nega")
                    step(dve.tensor_tensor(g["y0"][:, :, :, :], g["y1"][:, :, :, :], g["y2"][:, :, :, :], ALU.add))
                    for d in range(2):
                        ins = dve.scalar_tensor_tensor(out=g["g"][:, d, :, :], in0=g["y0"][:, d, :, :], scalar=-1.0,
                                                       in1=bc(nega[:, 8 * d:8 * d + 8], 1, NT), op0=ALU.mult,
                                                       op1=ALU.mult)
                    ins.then_inc(done, 1)
                elif kind == "nbe":
                    s, = key
                    g = gates_[s]
                    need(dve, "bsig", s)
                    need(dve, "eall", s)
                    step(dve.tensor_scalar(g["nbeta"][:, :, :, :], g["beta"][:, :, :, :], -1.0, None, ALU.mult))
                    dve.tensor_tensor(g["y0"][:, :, :, :], g["nbeta"][:, :, :, :], ex[s][:, 0, :, :, :],
                                      ALU.mult).then_inc(done, 1)
                elif kind in ("tapa", "taps"):
                    n = conv_cus.index(key)
                    what, s, p = key
                    h = 0 if kind == "tapa" else 1
                    need(dve, "tap2", *key)
                    pr = projection(dve, key)
                    for tap in (0, 1, 3, 4):
                        off = tap - W5 // 2
                        a, b = max(0, -off), T - max(0, off)
                        col = VC_C5 + tap * 24 + CU_TILE[what] + 2 * p + h
                        o = sil[:, n % 2, h, a:b]
                        ins = dve.scalar_tensor_tensor(out=o, in0=pr[:, T * h + a + off:T * h + b + off],
                                                       scalar=vcol[:, col:col + 1], in1=o, op0=ALU.mult, op1=ALU.add)
                        if tap != 4:
                            step(ins)
                    ins.then_inc(done, 1)
                elif kind == "nsq":
                    s, what, p = key
                    need(dve, "natc", what, s, p)
                    before = PAIRS[PAIRS.index((s, p)) - 1]
                    if what == "q":
                        need(dve, "nsq", s, "k", p)
                    elif (s, p) == PAIRS[0]:
                        need(dve, "hlo", LAT, 7)
                    elif before[0] == CTX:
                        need(dve, "st", *before, 1)
                    else:
                        need(dve, "mix_hi", before[1])
                        need(dve, "mix_lo", before[1])
                    a = 8 if what == "k" else 12
                    kq = kvq[what][:, PAIRS.index((s, p)) % 2, :, :, :].rearrange("p t h d -> p (t h) d")
                    step(dve.tensor_tensor(four(tmp), kq, kq, ALU.mult))
                    dve.tensor_reduce(sums[:, a:a + 4], four(tmp), AX_X, ALU.add).then_inc(done, 1)
                elif kind == "nrc":
                    need(dve, "nrt", *key)
                    a = 8 if key[1] == "k" else 12
                    dve.reciprocal(rstd[:, a:a + 4], rtmp[:, a:a + 4]).then_inc(done, 1)
                elif kind == "kn":
                    s, what, p = key
                    need(dve, "nrc", *key)
                    a = 8 if what == "k" else 12
                    kq = kvq[what][:, PAIRS.index((s, p)) % 2, :, :, :].rearrange("p t h d -> p (t h) d")
                    dve.tensor_tensor(kq, kq, bc(rstd[:, a:a + 4], 2, P), ALU.mult).then_inc(done, 1)
                elif kind == "gk":
                    s, p, t = key
                    n = 4 if s == LAT else 2
                    need(dve, "kk", *key)
                    need(dve, "edec", *key)
                    e = e_[:, 0:n, :].rearrange("p a b -> p (a b)")
                    dve.tensor_tensor(e, PS[:, BANK["kk", key], 0:n * P], e, ALU.mult).then_inc(done, 1)
                elif kind == "mneg":
                    s, p, t = key
                    need(dve, "gk", *key)
                    need(dve, "nbe", s)
                    k = PAIRS.index((s, p))
                    if k:
                        need(dve, "vn", *PAIRS[k - 1], 1)
                    for d, m in enumerate((m_gt, m_lt)):
                        for h in range(2):
                            ins = dve.scalar_tensor_tensor(
                                out=mn[:, t, 2 * d + h, :], in0=e_[:, h, :],
                                scalar=gates_[s]["nbeta"][:, d, t, 2 * p + h:2 * p + h + 1], in1=m[:, :],
                                op0=ALU.mult, op1=ALU.mult)
                    ins.then_inc(done, 1)
                elif kind == "xadd":
                    s, p, t, l = key
                    buf = xi[:, t, :, :]
                    if l == 0:
                        need(dve, "z", *key)
                        k = PAIRS.index((s, p))
                        if k:
                            need(dve, "nx", *PAIRS[k - 1], t)
                        dve.tensor_tensor(buf, four(PS[:, BANK["z", key], :]), bc(ident[:, :], 1, 4),
                                          ALU.add).then_inc(done, 1)
                    else:
                        need(dve, "xy", *key)
                        need(dve, "xadd", s, p, t, l - 1)
                        dve.tensor_tensor(buf, four(PS[:, BANK["xy", key, "x"], :]), buf.bitcast(F32),
                                          ALU.add).then_inc(done, 1)
                elif kind == "yone":
                    s, p, t = key
                    need(dve, "mk", s, p, t, 0)
                    k = PAIRS.index((s, p))
                    if k:
                        need(dve, "nx", *PAIRS[k - 1], t)
                    dve.tensor_tensor(yi[:, t, :, :], mkl[:, t, :, :].bitcast(F32), bc(ident[:, :], 1, 4),
                                      ALU.add).then_inc(done, 1)
                elif kind == "nrr":
                    t = key[2]
                    need(dve, "nr", *key)
                    dve.tensor_tensor(zi[:, t, :, :], four(PS[:, BANK["nr", key], :]), bc(ident[:, :], 1, 4),
                                      ALU.add).then_inc(done, 1)
                elif kind == "xf":
                    t = key[2]
                    need(dve, "nx", *key)
                    dve.tensor_tensor(mn[:, t, :, :], four(PS[:, BANK["nx", key], :]), xi[:, t, :, :].bitcast(F32),
                                      ALU.add).then_inc(done, 1)
                elif kind == "r":
                    s, p, i = key
                    need(dve, "ks", *key)
                    need(dve, "vb", *key)
                    for d in range(2):
                        for h in range(2):
                            n = 2 * d + h
                            ins = dve.scalar_tensor_tensor(
                                out=rb[:, n, :], in0=PS[:, BANK["ks", key], P * n:P * (n + 1)],
                                scalar=gates_[s]["y0"][:, d, tile_of(d, i), 2 * p + h:2 * p + h + 1],
                                in1=rb[:, n, :], op0=ALU.mult, op1=ALU.add)
                    ins.then_inc(done, 1)
                elif kind == "stc":
                    s, p, i = key
                    need(dve, "st", *key)
                    ps = PS[:, BANK["st", key], :]
                    if s == CTX and i == 0:
                        dve.tensor_copy(sctx[:, p, :, :], four(ps)).then_inc(done, 1)
                        continue
                    if s == CTX:
                        need(dve, "stc", s, p, 0)
                    elif p:
                        need(dve, "o", p - 1)
                    new = sctx[:, p, :, :] if s == CTX else slat[:, :, :]
                    for d in range(2):
                        for h in range(2):
                            n = 2 * d + h
                            ins = dve.scalar_tensor_tensor(
                                out=new[:, n, :], in0=sctx[:, p, n, :],
                                scalar=ex[s][:, 2, d, tile_of(d, i), 2 * p + h:2 * p + h + 1],
                                in1=ps[:, P * n:P * (n + 1)], op0=ALU.mult, op1=ALU.add)
                    ins.then_inc(done, 1)
                elif kind == "osq":
                    need(dve, "oc", *key)
                    step(dve.tensor_tensor(four(tmp), rb[:, :, :], rb[:, :, :], ALU.mult))
                    dve.tensor_reduce(sums[:, 8:12], four(tmp), AX_X, ALU.add).then_inc(done, 1)
                elif kind == "orc":
                    need(dve, "ort", *key)
                    dve.reciprocal(rstd[:, 8:12], rtmp[:, 8:12]).then_inc(done, 1)
                elif kind == "on":
                    need(dve, "orc", *key)
                    dve.tensor_tensor(rb[:, :, :], rb[:, :, :], bc(rstd[:, 8:12], 2, P), ALU.mult).then_inc(done, 1)
                elif kind == "ym":
                    p, = key
                    need(dve, "oT", p)
                    need(dve, "zsilu", "z", LAT, p)
                    ps = PS[:, BANK["oT", key], :].rearrange("p (t h c) -> p t h c", t=NT, h=2)
                    y = kd[:, :, :].rearrange("p (h t) c -> p h t c", h=2)
                    for h in range(2):
                        ins = dve.scalar_tensor_tensor(
                            out=y[:, h, :, :], in0=ps[:, :, h, :], scalar=vcol[:, VC_ON:VC_ON + 1],
                            in1=zs[:, p % 2, h, :].rearrange("p (t c) -> p t c", t=NT), op0=ALU.mult, op1=ALU.mult)
                    ins.then_inc(done, 1)
                elif kind == "mix_lo":
                    n, = key
                    need(dve, "mix_hi", n)
                    src = kd[:, :, :].rearrange("p a b -> p (a b)") if n < NP else ub[:, :]
                    dve.tensor_tensor(hc_lo[:, 2 * n:2 * n + 2, :].rearrange("p a b -> p (a b)"), src,
                                      hc_hi[:, 2 * n:2 * n + 2, :].bitcast(F32).rearrange("p a b -> p (a b)"),
                                      ALU.subtract).then_inc(done, 1)
                elif kind == "u":
                    i, = key
                    need(dve, "sg", i)
                    if i:
                        need(dve, "dw", i - 1, NDW - 1)
                    dve.tensor_tensor(ub[:, :], projection(dve, ("a", LAT, i)), sgb[:, :], ALU.mult).then_inc(done, 1)
                elif kind == "dw":
                    i, n = key
                    taps = [k for k in range(W31) if k != W31 // 2][2 * n:2 * n + 2]
                    if n == 0:
                        need(dve, "u", i)
                        taps = [W31 // 2] + taps
                    else:
                        need(dve, "dw", i, n - 1)
                    for tap in taps:
                        off = tap - W31 // 2
                        a, b = max(0, -off), ROW - max(0, off)
                        for h in range(2):
                            col = VC_C31 + tap * 8 + 2 * i + h
                            src = ub[:, T * h:T * (h + 1)].rearrange("p (r w) -> p r w", w=ROW)[:, :, a + off:b + off]
                            dst = cacc[:, 2 * i + h, :].rearrange("p (r w) -> p r w", w=ROW)[:, :, a:b]
                            if off == 0:
                                ins = dve.tensor_scalar(dst, src, vcol[:, col:col + 1], None, ALU.mult)
                            else:
                                ins = dve.scalar_tensor_tensor(out=dst, in0=src, scalar=vcol[:, col:col + 1],
                                                               in1=dst, op0=ALU.mult, op1=ALU.add)
                            if (tap, h) != (taps[-1], 1):
                                step(ins, 1)
                    ins.then_inc(done, 1)
                elif kind == "cen":
                    need(dve, "lnm")
                    dve.scalar_tensor_tensor(out=cacc[:, :, :], in0=bc(PS[:, BANK["lnm", ()], 0:T], 1, 8),
                                             scalar=-1.0 / DC, in1=cacc[:, :, :], op0=ALU.mult,
                                             op1=ALU.add).then_inc(done, 1)
                elif kind == "lva":
                    i, = key
                    need(dve, "lnv", i)
                    ps = PS[:, BANK["lnv", key], 0:T]
                    if i == 0:
                        dve.tensor_copy(cx[:, 0, :], ps).then_inc(done, 1)
                    else:
                        need(dve, "lva", i - 1)
                        dve.tensor_tensor(cx[:, 0, :], ps, cx[:, 0, :], ALU.add).then_inc(done, 1)
                elif kind == "lnr":
                    need(dve, "lsd")
                    dve.reciprocal(cx[:, 0, :], cx[:, 1, :]).then_inc(done, 1)
                elif kind == "lnn":
                    need(dve, "lnr")
                    dve.tensor_tensor(cacc[:, :, :], cacc[:, :, :], bc(cx[:, 0, :], 1, 8), ALU.mult).then_inc(done, 1)
                elif kind == "macc":
                    m, j = key
                    n = at_ring["mr", m, j]
                    dve.wait_ge(landed[n % RING], 16 * (n // RING + 1))
                    if j == 0:
                        need(dve, "csil")
                        if m >= 2:
                            need(dve, "mcol", m - 2)
                        step(dve.tensor_scalar(macc[:, m % 2, :], raw[:, n % RING, 0:512], csil[:, LAT, 0:1], None, ALU.mult))
                    else:
                        need(dve, "macc", m, j - 1)
                        step(dve.scalar_tensor_tensor(out=macc[:, m % 2, :], in0=raw[:, n % RING, 0:512],
                                                      scalar=csil[:, LAT, 2 * j:2 * j + 1], in1=macc[:, m % 2, :],
                                                      op0=ALU.mult, op1=ALU.add))
                    dve.scalar_tensor_tensor(out=macc[:, m % 2, :], in0=raw[:, n % RING, 512:1024],
                                             scalar=csil[:, LAT, 2 * j + 1:2 * j + 2], in1=macc[:, m % 2, :],
                                             op0=ALU.mult, op1=ALU.add).then_inc(done, 1)
                elif kind == "mcc":
                    m, = key
                    need(dve, "mcol", m)
                    dve.tensor_tensor(modc[:, 4 * m:4 * m + 4], PS[:, BANK["mcol", key], 0:4],
                                      vcol[:, VC_MOD + 4 * m:VC_MOD + 4 * m + 4], ALU.add).then_inc(done, 1)
                elif kind == "gdiag" and key[0] == 0:
                    gate_diagonal(*key)
                elif kind == "yg":
                    t, c = key
                    need(dve, "ysq", *key)
                    need(dve, "gbc", 0, c)
                    b = PS[:, 2 * c + t, :]
                    dve.tensor_tensor(b, b, gw_all[:, 512 * c:512 * (c + 1)], ALU.mult).then_inc(done, 1)
                elif kind in ("ysm", "psm"):
                    need(dve, "ysq" if kind == "ysm" else "psq", 1, 3)
                    a, o = (8, 6) if kind == "ysm" else (16, 4)
                    dve.tensor_reduce(sums[:, o:o + 2], sums[:, a:a + 8].rearrange("p (t c) -> p t c", t=NT), AX_X,
                                      ALU.add).then_inc(done, 1)
                elif kind == "yrc":
                    need(dve, "yrt")
                    dve.reciprocal(rstd[:, 6:8], rtmp[:, 6:8]).then_inc(done, 1)
                elif kind == "pn":
                    t, c = key
                    need(dve, "yrc")
                    need(dve, "yg", t, c)
                    dve.wait_ge(x_again, 16)
                    xc = x1[:, t, 512 * c:512 * (c + 1)]
                    dve.scalar_tensor_tensor(out=xc, in0=PS[:, 2 * c + t, :], scalar=rstd[:, 6 + t:7 + t], in1=xc,
                                             op0=ALU.mult, op1=ALU.add).then_inc(done, 1)

            def split(n, count):
                dve.wait_ge(S["hi"], count)
                slot = (B0 + n) % RING
                dve.tensor_tensor(w_lo[:, slot, :], raw[:, (R0 + n) % RING, :], w_hi[:, slot, :].bitcast(F32),
                                  ALU.subtract).then_inc(S["lo"], 1)

            def product(c, static):
                dve.wait_ge(f_mm, c * 16)
                dve.wait_ge(f_sg, c)
                if not (static and c < 2):
                    dve.wait_ge(f_tr, c - 1)
                dve.tensor_tensor(anf[:, :, :], PS[:, 2:4, :], sgf[:, :, :], ALU.mult).then_inc(f_an, 1)

            def turned_lo(cs, c1, ah):
                dve.wait_ge(f_ah, ah)
                for t in range(NT):
                    dve.tensor_tensor(act_lo[:, cs, P * t:P * (t + 1)], four(PS[:, 4 + t, :]),
                                      act_hi[:, cs, P * t:P * (t + 1)].bitcast(F32), ALU.subtract).then_inc(f_al, 1)

            def gate_up(c, static):
                for i in range(16):
                    split(i, c * 16 + (B0 + i + 1))
                    if static and c == 0:
                        if 2 <= i < 6:
                            gate_diagonal(1, i - 2)
                        continue
                    if i == 3:
                        product(c, static)
                    if i == 9:
                        turned_lo(slice(4 * (c - 1), 4 * c) if static else ds(c * 4 - 4, 4), c, c * 2)

            gate_up(0, True)
            gate_up(1, True)
            with dve.Fori(2, FC) as c:
                gate_up(c, False)
            for v in range(ND):
                split(NG + v, B0 + NG + v + 1)
                if v == 1:
                    product(FC, True)
                if v == 4:
                    turned_lo(slice(4 * (FC - 1), 4 * FC), FC, 2 * FC)
                if v in (30, 52, 74):
                    cc = v // 22 - 1
                    dve.wait_ge(f_sq, 2 * cc + 2)
                    for t in range(NT):
                        b = PS[:, 2 * cc + t, :]
                        dve.tensor_tensor(b, b, gw_all[:, 512 * cc:512 * (cc + 1)], ALU.mult).then_inc(f_yg, 1)
            dve.wait_ge(f_sq, 8)
            dve.tensor_reduce(rtmp[:, 2:4], sums[:, 8:16].rearrange("p (t c) -> p t c", t=NT), AX_X,
                              ALU.add).then_inc(f_rc, 1)
            for t in range(NT):
                b = PS[:, 6 + t, :]
                dve.tensor_tensor(b, b, gw_all[:, 1536:2048], ALU.mult).then_inc(f_yg, 1)
            dve.wait_ge(f_rt, 1)
            step(dve.reciprocal(rstd[:, 0:2], rtmp[:, 0:2]))
            dve.wait_ge(f_yg, 8)
            for t in range(NT):
                for cc in range(4):
                    xc = x1[:, t, 512 * cc:512 * (cc + 1)]
                    dve.scalar_tensor_tensor(out=xc, in0=PS[:, 2 * cc + t, :], scalar=rstd[:, t:t + 1], in1=xc,
                                             op0=ALU.mult, op1=ALU.add).then_inc(f_out, 1)

        @block.tensor
        def _(pe):
            def product(out_ap, a, b, cols, start, stop, grouped=False):
                for n, (i, j) in enumerate(((0, 0), (0, 1), (1, 0))):
                    ins = pe.matmul(out_ap, a[i], b[j], start=start and n == 0, stop=stop and n == 2,
                                    skip_group_check=grouped)
                return ins

            def turn4(bank_, srcs):
                for n, src in enumerate(srcs):
                    ins = pe.transpose(PS[:, bank_, P * n:P * (n + 1)], src, ident[:, :])
                return ins

            def gate_sum(w, q):
                need(pe, "gdiag", w, q)
                b = aux(pe, "gb", (w, q))
                pe.matmul(PS[:, b, :], ones[:, :], sgf[:, 0, :], start=True, stop=True).then_inc(S["gb"], 1)

            for kind, key in PLAN:
                done = S[kind]
                if kind == "vT":
                    n, = key
                    need(pe, "masks")
                    pe.wait_ge(small_in["vec"], 16 * 11)
                    b = aux(pe, kind, key)
                    for v, rows, col in (((0, 81, 0), (1, 64, 128), (2, 120, 256)), ((3, 124, 0), (4, 124, 124)))[n]:
                        ins = pe.transpose(PS[:, b, col:col + rows], vnat[0:rows, v, :], ident[0:rows, 0:rows])
                    ins.then_inc(done, 1)
                elif kind == "mm":
                    u, half = key
                    if half == 0:
                        need(pe, "hi", u)
                        need(pe, "lo", u)
                    hi, lo = wide(u, unit_size(u))
                    if u[0] == "mod":
                        _, hf, j, q = u
                        if (hf, j, q) == (0, 0, 0):
                            need(pe, "c4l")
                        if (hf, j, q) == (1, 0, 0):
                            need(pe, "mrow", 0)
                        for n in range(2):
                            for m, w in enumerate((hi, lo)):
                                ins = pe.matmul(PS[0:4, 2 * q + n, :], c4[:, j, :], w[:, 512 * n:512 * (n + 1)],
                                                start=j == 0 and m == 0, stop=j == KT - 1 and m == 1)
                    elif u[0] == "ba":
                        s = u[1]
                        b = proj_bank[u]
                        need(pe, "mrow", 1)
                        need(pe, "hlo", s, 7)
                        for r in ([] if projected.index(u) < 4 else first_read(projected[projected.index(u) - 4])):
                            need(pe, r[0], *r[1])
                        hh, hl = seq_h[s]
                        for t in range(NT):
                            for kt in range(KT):
                                tok, col = slice(P * t, P * (t + 1)), slice(32 * kt, 32 * kt + 32)
                                ins = product(PS[:, b, 32 * t:32 * t + 32], (hh[:, kt, tok], hl[:, kt, tok]),
                                              (hi[:, col], lo[:, col]), 32, kt == 0, kt == KT - 1)
                    elif u[0] == "win":
                        cu, g = u[1:]
                        s = cu[1]
                        b = proj_bank[cu]
                        if (g, half) == (0, 0):
                            k = projected.index(cu)
                            for r in first_read(projected[k - 4]) if k >= 4 else []:
                                need(pe, r[0], *r[1])
                            need(pe, "mrow", 1)
                        hh, hl = seq_h[s]
                        for k in range(2):
                            kt = 4 * g + 2 * half + k
                            if k == 0:
                                need(pe, "hlo", s, kt // 2)
                            for h in range(2):
                                col = slice(256 * (2 * half + k) + P * h, 256 * (2 * half + k) + P * (h + 1))
                                ins = product(PS[:, b, T * h:T * (h + 1)], (hi[:, col], lo[:, col]),
                                              (hh[:, kt, :], hl[:, kt, :]), T, kt == 0 and h == 0, kt == KT - 1, True)
                    else:
                        _, cc, kg = u
                        kt = 2 * kg + half
                        need(pe, "mix_lo", NP + (kt - 8) // 2 if kt >= 8 else kt // 2)
                        if (kg, half) == (4, 0):
                            if cc < 2:
                                for w in projected[-4:]:
                                    for r in first_read(w):
                                        need(pe, r[0], *r[1])
                            else:
                                need(pe, "gbc", 0, 3)
                        for t in range(NT):
                            tok, col = slice(P * t, P * (t + 1)), slice(512 * half, 512 * (half + 1))
                            ins = product(PS[:, 2 * cc + t, :], (hc_hi[:, kt, tok], hc_lo[:, kt, tok]),
                                          (hi[:, col], lo[:, col]), 512, (kg, half) == (4, 0), (kg, half) == (3, 1))
                    ins.then_inc(done, 1)
                elif kind == "modcol":
                    need(pe, "mrow", 1)
                    pe.wait_ge(small_in["bmod"], 16)
                    b = aux(pe, kind, key)
                    for n in range(2 * KT):
                        ins = pe.matmul(PS[:, b, 2 * n:2 * n + 2], modrow[0:5, P * n:P * (n + 1)], sel[0:5, :],
                                        start=True, stop=True)
                    ins.then_inc(done, 1)
                elif kind == "xT":
                    s, kp = key
                    b = aux(pe, kind, key)
                    if s == FFN:
                        need(pe, "xdg")
                        need(pe, "pn", 1, 3)
                        for n in range(4):
                            k, t = divmod(n, 2)
                            ins = pe.matmul(PS[:, b, P * n:P * (n + 1)],
                                            x1[:, t, P * (2 * kp + k):P * (2 * kp + k + 1)], dg[:, t, :],
                                            start=True, stop=True)
                        ins.then_inc(done, 1)
                        continue
                    else:
                        need(pe, "xn", s, 1)
                        need(pe, "xsq", LAT, 1)
                        src = xs[s]
                    turn4(b, [src[:, t, P * (2 * kp + k):P * (2 * kp + k + 1)] for k in range(2) for t in range(NT)])\
                        .then_inc(done, 1)
                elif kind == "pref":
                    s, = key
                    need(pe, "gg", s)
                    b = aux(pe, kind, key)
                    for k, ms in enumerate(((m_le, m_ge), (m_gt, m_lt), (ones, ones))):
                        for d in range(2):
                            ins = pe.matmul(PS[:, b, 16 * (2 * k + d):16 * (2 * k + d + 1)], ms[d][:, :],
                                            gates_[s]["g"][:, d, :, :].rearrange("p t h -> p (t h)"),
                                            start=True, stop=True)
                    ins.then_inc(done, 1)
                elif kind == "nat":
                    n = conv_cus.index(key)
                    need(pe, "csilu", *key)
                    b = aux(pe, kind, key)
                    turn4(b, [sil[:, n % 2, h, P * t:P * (t + 1)] for t in range(NT) for h in range(2)])\
                        .then_inc(done, 1)
                elif kind in ("kT", "qT"):
                    if kind == "kT":
                        s, p = key
                        need(pe, "kn", s, "k", p)
                        src = kvq["k"][:, PAIRS.index((s, p)) % 2, :, :, :]
                    else:
                        p, k = key
                        need(pe, "kn", LAT, "q", p)
                        if k:
                            need(pe, "qdec", p, k)
                        src = qx[:, :, :, :] if k else kvq["q"][:, PAIRS.index((LAT, p)) % 2, :, :, :]
                    b = aux(pe, kind, key)
                    turn4(b, [src[:, t, h, :] for t in range(NT) for h in range(2)]).then_inc(done, 1)
                elif kind == "dec":
                    s, p, t, k = key
                    need(pe, "gm", *key)
                    b = BANK["dec", (s, p, t, 0)] if k else aux(pe, kind, key)
                    for d, m in enumerate(((m_le, m_ge), (m_gt, m_lt))[k]):
                        ins = pe.matmul(PS[:, b, T * k:T * (k + 1)], m[:, :],
                                        gmv[:, d, :, :].rearrange("p h c -> p (h c)"), start=d == 0, stop=d == 1)
                    ins.then_inc(done, 1)
                elif kind == "kk":
                    s, p, t = key
                    need(pe, "kTc", s, p)
                    if s == LAT:
                        need(pe, "qTc", p, 0)
                    b = aux(pe, kind, key)
                    for n in range(4 if s == LAT else 2):
                        rhs = kTs[:, t, n, :] if n < 2 else qTs[:, 0, t, n - 2, :]
                        ins = pe.matmul(PS[:, b, P * n:P * (n + 1)], kTs[:, t, n % 2, :], rhs, start=True, stop=True)
                    ins.then_inc(done, 1)
                elif kind == "z":
                    s, p, t, l = key
                    need(pe, "mk", *key)
                    if l:
                        need(pe, "xadd", s, p, t, l - 1)
                    else:
                        need(pe, "cst")
                    b = aux(pe, kind, key)
                    for n in range(4):
                        ins = pe.matmul(PS[:, b, P * n:P * (n + 1)], mkl[:, t, n, :],
                                        xi[:, t, n, :] if l else id_r[:, :], start=True, stop=True)
                    ins.then_inc(done, 1)
                elif kind == "xy":
                    s, p, t, l = key
                    need(pe, "zc", *key)
                    need(pe, *(("yadd", s, p, t, l - 1) if l > 1 else ("yone", s, p, t)))
                    bx, by = aux(pe, kind, key, "x"), aux(pe, kind, key, "y")
                    for n in range(4):
                        pe.matmul(PS[:, bx, P * n:P * (n + 1)], yi[:, t, n, :], zi[:, t, n, :], start=True, stop=True)
                    pe.matmul(PS[:, by, :], id_r[:, :], yi[:, t, :, :].rearrange("p a b -> p (a b)"), start=True,
                              stop=False, skip_group_check=True)
                    for n in range(4):
                        ins = pe.matmul(PS[:, by, P * n:P * (n + 1)], zi[:, t, n, :], yi[:, t, n, :], start=False,
                                        stop=n == 3, skip_group_check=True)
                    ins.then_inc(done, 1)
                elif kind == "nr":
                    s, p, t = key
                    need(pe, "mlo", *key)
                    need(pe, "xadd", s, p, t, LEVELS - 1)
                    b = aux(pe, kind, key)
                    pe.matmul(PS[:, b, :], nid_r[:, :], xi[:, t, :, :].rearrange("p a b -> p (a b)"), start=True,
                              stop=False, skip_group_check=True)
                    for n in range(4):
                        for k, w in enumerate((mhi[:, t, n, :], mkl[:, t, n, :])):
                            ins = pe.matmul(PS[:, b, P * n:P * (n + 1)], w, xi[:, t, n, :], start=False,
                                            stop=(n, k) == (3, 1), skip_group_check=True)
                    ins.then_inc(done, 1)
                elif kind == "nx":
                    s, p, t = key
                    need(pe, "nrr", *key)
                    need(pe, "yadd", s, p, t, LEVELS - 1)
                    b = aux(pe, kind, key)
                    for n in range(4):
                        ins = pe.matmul(PS[:, b, P * n:P * (n + 1)], yi[:, t, n, :], zi[:, t, n, :],
                                        start=True, stop=True)
                    ins.then_inc(done, 1)
                elif kind in ("ks", "vn", "st"):
                    s, p, i = key
                    if kind == "ks":
                        need(pe, "kTc", s, p)
                        need(pe, "stc", *((s, p, 0) if i else (CTX, p, 1)))
                        state = slat if (s, i) == (LAT, 1) else sctx[:, p, :, :]
                    elif kind == "vn":
                        need(pe, "xf", s, p, 1)
                        need(pe, "vb", *key)
                        if ("r", key) in COUNT:
                            need(pe, "r", *key)
                    else:
                        need(pe, "kd", *key)
                        need(pe, "vnc", *key)
                    b = aux(pe, kind, key)
                    for d in range(2):
                        for h in range(2):
                            n, t = 2 * d + h, tile_of(d, i)
                            if kind == "ks":
                                a, m = kTs[:, t, h, :], state[:, n, :]
                            elif kind == "vn":
                                a, m = mn[:, t, n, :], rb[:, n, :]
                            else:
                                a, m = kd[:, n, :], vnew[:, i, n, :]
                            ins = pe.matmul(PS[:, b, P * n:P * (n + 1)], a, m, start=True, stop=True)
                    ins.then_inc(done, 1)
                elif kind == "o":
                    p, = key
                    need(pe, "qTc", p, 2)
                    need(pe, "vnc", LAT, p, 1)
                    need(pe, "attn", p, 1)
                    b = aux(pe, kind, key)
                    for t in range(NT):
                        for h in range(2):
                            for d in range(2):
                                i = tile_of(d, t)
                                state = slat if i else sctx[:, p, :, :]
                                o = PS[:, b, P * (2 * t + h):P * (2 * t + h + 1)]
                                pe.matmul(o, qTs[:, 1 + d, t, h, :], state[:, 2 * d + h, :], start=d == 0, stop=False)
                                ins = pe.matmul(o, at[:, t, d, h, :], vnew[:, i, 2 * d + h, :], start=False,
                                                stop=d == 1)
                    ins.then_inc(done, 1)
                elif kind == "oT":
                    need(pe, "on", *key)
                    b = aux(pe, kind, key)
                    turn4(b, [rb[:, n, :] for n in range(4)]).then_inc(done, 1)
                elif kind == "lnm":
                    need(pe, "dw", 3, NDW - 1)
                    b = aux(pe, kind, key)
                    for n in range(8):
                        ins = pe.matmul(PS[:, b, 0:T], ones[:, :], cacc[:, n, :], start=n == 0, stop=n == 7)
                    ins.then_inc(done, 1)
                elif kind == "lnv":
                    need(pe, "csq", *key)
                    b = aux(pe, kind, key)
                    for n in range(2):
                        ins = pe.matmul(PS[:, b, 0:T], ones[:, :], ub[:, T * n:T * (n + 1)], start=n == 0, stop=n == 1)
                    ins.then_inc(done, 1)
                elif kind == "mcol":
                    m, = key
                    need(pe, "macc", m, 7)
                    b = aux(pe, kind, key)
                    for n in range(4):
                        ins = pe.matmul(PS[:, b, n:n + 1], macc[:, m % 2, P * n:P * (n + 1)], ones[:, 0:1],
                                        start=True, stop=True)
                    ins.then_inc(done, 1)
                elif kind == "gb" and key[0] == 0:
                    gate_sum(*key)

            def unit(slot, ready, k0, left, banks, first, last):
                pe.wait_ge(S["hi"], ready)
                pe.wait_ge(S["lo"], ready)
                for k in range(2):
                    col = slice(512 * k, 512 * (k + 1))
                    for t in range(NT):
                        tok = slice(P * t, P * (t + 1))
                        ins = product(PS[:, banks + t, :], (left[0][:, k0 + k, tok], left[1][:, k0 + k, tok]),
                                      (w_hi[:, slot, col], w_lo[:, slot, col]), 512, first and k == 0, last and k == 1)
                ins.then_inc(f_mm, 1)

            def turn(c, static):
                pe.wait_ge(f_an, c)
                if static and c == 1:
                    need(pe, "gbc", 1, 3)
                else:
                    pe.wait_ge(f_al, c * 2 - 2)
                for t in range(NT):
                    ins = turn4(4 + t, [anf[:, t, P * f:P * (f + 1)] for f in range(4)])
                ins.then_inc(f_tr, 1)

            def gate_up(c, static):
                for i in range(16):
                    if static and c == 0:
                        if i < 8:
                            need(pe, "flo", FFN, i)
                    elif i == 0:
                        pe.wait_ge(f_sg, c)
                    elif i == 8:
                        pe.wait_ge(f_an, c)
                    unit((B0 + i) % RING, c * 16 + (B0 + i + 1), 2 * (i % 8), (h_hi, h_lo), 0 if i < 8 else 2,
                         i % 8 == 0, i % 8 == 7)
                    if static and c == 0 and 3 <= i < 7:
                        gate_sum(1, i - 3)
                    if i == 5 and not (static and c == 0):
                        turn(c, static)

            gate_up(0, True)
            gate_up(1, True)
            with pe.Fori(2, FC) as c:
                gate_up(c, False)
            for v in range(ND):
                cc, g = divmod(v, FT // 2)
                if v == 0:
                    pe.wait_ge(f_sg, FC)
                    pe.wait_ge(f_al, 2 * FC - 2)
                if v == 20:
                    pe.wait_ge(f_al, 2 * FC)
                unit((B0 + NG + v) % RING, B0 + NG + v + 1, 2 * g, (act_hi, act_lo), 2 * cc, g == 0,
                     g == FT // 2 - 1)
                if v == 2:
                    turn(FC, True)


_INS = ["x", "c", "ctx", "c_ctx", "w_mod", "b_mod", "mix_norm_pre", "mix_norm_post", "w_in", "qkv_conv", "a_log",
        "dt_bias", "delta_out_norm", "conf_dw", "conf_ln_w", "conf_ln_b", "w_out", "ffn_norm_pre", "ffn_norm_post",
        "w_gate", "w_up", "w_down"]


def kernel(**inputs):
    import numpy as np
    import concourse.bacc as bacc
    from concourse.bass_utils import run_bass_kernel_spmd

    nc = bacc.Bacc("TRN2", target_bir_lowering=False, num_devices=1)
    arrays, args = {}, []
    for name in _INS:
        a = np.ascontiguousarray(inputs[name])
        arrays[f"in_{name}_dram"] = a
        args.append(nc.dram_tensor(f"in_{name}_dram", a.shape, mybir.dt.from_np(a.dtype), kind="ExternalInput").ap())
    args.append(nc.dram_tensor("out_dram", (1, T, D), F32, kind="ExternalOutput").ap())
    layer(nc, *args)
    return run_bass_kernel_spmd(nc, [arrays], core_ids=[0]).results[0]["out_dram"]
```
